# Optimizing a Trainium2 kernel written in Bass

```python
import math
import jax, jax.numpy as jnp
from jax import lax
import numpy as np

D_MODEL = 2048
BATCH = 1
SEQ = 256
DEPTH = 2
DEC_BATCH = 8
DEC_SEQ = 4
PAST_LEN = 2048
PAGE_SIZE = 128

MIX_WIDTH = D_MODEL
SWA_WIDTH = MIX_WIDTH // 2
RET_WIDTH = MIX_WIDTH - SWA_WIDTH
SWA_HEADS = 8
SWA_KV_HEADS = 2
SWA_HEAD_DIM = SWA_WIDTH // SWA_HEADS
WINDOW = 128
BLOCK = WINDOW
RET_HEADS = 4
RET_KEY_DIM = RET_WIDTH // RET_HEADS
RET_VAL_DIM = RET_WIDTH // RET_HEADS
RET_CHUNK = 128
ROPE_BASE = 10000.0
N_BUCKETS = 32
MAX_DISTANCE = 128
EPS = 1e-6
_FF_RAW = -(-8 * D_MODEL // 3)
D_FF = -(-_FF_RAW // 256) * 256

_SEG = (SWA_HEADS * SWA_HEAD_DIM, SWA_KV_HEADS * SWA_HEAD_DIM, SWA_KV_HEADS * SWA_HEAD_DIM,
        RET_HEADS * RET_KEY_DIM, RET_HEADS * RET_KEY_DIM, RET_HEADS * RET_VAL_DIM, RET_WIDTH)
IN_COLS = sum(_SEG)
SPLITS = tuple(int(s) for s in np.cumsum(_SEG)[:-1])

kernel_name = "hymba_swa_sink_retention_decode_step"

def _rmsnorm(x, g):
    xf = x.astype(jnp.float32)
    y = xf * lax.rsqrt(jnp.mean(xf * xf, axis=-1, keepdims=True) + EPS)
    return (y * g.astype(jnp.float32)).astype(x.dtype)

def _t5_bucket(dist):
    n = jnp.maximum(dist, 0)
    max_exact = N_BUCKETS // 2
    nf = jnp.maximum(n, 1).astype(jnp.float32)
    large = max_exact + (jnp.log(nf / max_exact) / math.log(MAX_DISTANCE / max_exact)
                         * (N_BUCKETS - max_exact)).astype(jnp.int32)
    large = jnp.minimum(large, N_BUCKETS - 1)
    return jnp.where(n < max_exact, n, large)

def _rotary(x, pos):
    half = x.shape[-1] // 2
    inv = 1.0 / (ROPE_BASE ** jnp.linspace(0.0, 1.0, half, dtype=jnp.float32))
    ang = pos.astype(jnp.float32)[:, None] * inv[None, :]
    cos = jnp.cos(ang)[None, :, None, :]
    sin = jnp.sin(ang)[None, :, None, :]
    xf = x.astype(jnp.float32)
    x1, x2 = xf[..., :half], xf[..., half:]
    return jnp.concatenate([x1 * cos - x2 * sin, x1 * sin + x2 * cos], axis=-1)

def _log_gamma():
    return jnp.log(1.0 - jnp.exp2(-5.0 - jnp.arange(RET_HEADS, dtype=jnp.float32)))

def _project(xn, w_in, pos):
    B, T, _ = xn.shape
    h = jnp.einsum('btd,dc->btc', xn, w_in)
    q_s, k_s, v_s, q_r, k_r, v_r, g_r = jnp.split(h, SPLITS, axis=-1)
    q_s = q_s.reshape(B, T, SWA_HEADS, SWA_HEAD_DIM)
    k_s = k_s.reshape(B, T, SWA_KV_HEADS, SWA_HEAD_DIM)
    v_s = v_s.reshape(B, T, SWA_KV_HEADS, SWA_HEAD_DIM)
    q_r = _rotary(q_r.reshape(B, T, RET_HEADS, RET_KEY_DIM), pos)
    k_r = _rotary(k_r.reshape(B, T, RET_HEADS, RET_KEY_DIM), pos) * (RET_KEY_DIM ** -0.5)
    v_r = v_r.reshape(B, T, RET_HEADS, RET_VAL_DIM).astype(jnp.float32)
    return q_s, k_s, v_s, q_r, k_r, v_r, g_r

def _swa_attend(q, k, v, q_pos, k_pos, sinks, rel_bias):
    B, NB, Q, H, hd = q.shape
    K = k.shape[2]
    G = H // SWA_KV_HEADS
    qg = q.reshape(B, NB, Q, SWA_KV_HEADS, G, hd)
    s = jnp.einsum('bnqkgd,bnjkd->bnkgqj', qg, k).astype(jnp.float32) * (hd ** -0.5)
    delta = q_pos[:, :, None] - k_pos[:, None, :]
    valid = (delta >= 0) & (delta < WINDOW) & (k_pos[:, None, :] >= 0)
    bias = rel_bias.astype(jnp.float32)[_t5_bucket(delta)]
    bias = bias.transpose(0, 3, 1, 2).reshape(NB, SWA_KV_HEADS, G, Q, K)
    s = jnp.where(valid[None, :, None, None], s + bias[None], -1e30)
    sink = sinks.astype(jnp.float32).reshape(SWA_KV_HEADS, G)[None, None, :, :, None, None]
    m = jnp.maximum(jnp.max(s, axis=-1, keepdims=True), sink)
    p = jnp.exp(s - m)
    p = p / (jnp.sum(p, axis=-1, keepdims=True) + jnp.exp(sink - m))
    o = jnp.einsum('bnkgqj,bnjkd->bnqkgd', p.astype(v.dtype), v)
    return o.reshape(B, NB, Q, H * hd)

def _retention_chunk(state, q, k, v):
    C = q.shape[1]
    lg = _log_gamma()
    idx = jnp.arange(C, dtype=jnp.float32)
    diff = idx[:, None] - idx[None, :]
    dmask = jnp.where(diff[None] >= 0, jnp.exp(jnp.maximum(diff, 0.0)[None] * lg[:, None, None]), 0.0)
    s = jnp.einsum('bnhd,bmhd->bhnm', q, k) * dmask[None]
    o = jnp.einsum('bhnm,bmhv->bnhv', s, v)
    q_decay = jnp.exp((idx[:, None] + 1.0) * lg[None, :])
    o = o + jnp.einsum('bnhd,bhdv->bnhv', q, state) * q_decay[None, :, :, None]
    k_decay = jnp.exp((C - 1.0 - idx)[:, None] * lg[None, :])
    new_state = (jnp.exp(C * lg)[None, :, None, None] * state
                 + jnp.einsum('bmhd,bmhv->bhdv', k * k_decay[None, :, :, None], v))
    return new_state, o

def _retention_prompt(q, k, v):
    B, S, H, dk = q.shape
    dv = v.shape[-1]
    nc = S // RET_CHUNK

    def to_chunks(a):
        return a.reshape(B, nc, RET_CHUNK, H, a.shape[-1]).transpose(1, 0, 2, 3, 4)

    s0 = jnp.zeros((B, H, dk, dv), jnp.float32)
    s_fin, o = lax.scan(lambda st, xs: _retention_chunk(st, *xs), s0,
                        (to_chunks(q), to_chunks(k), to_chunks(v)))
    o = o.transpose(1, 0, 2, 3, 4).reshape(B, S, H, dv)
    return o, s_fin

def _mix_out(x, o_swa, o_ret, g_r, w_o):
    B, T = x.shape[:2]
    o_ret = o_ret * lax.rsqrt(jnp.mean(o_ret * o_ret, axis=-1, keepdims=True) + EPS)
    o_ret = o_ret.reshape(B, T, RET_WIDTH) * jax.nn.silu(g_r.astype(jnp.float32))
    cat = jnp.concatenate([o_swa.astype(x.dtype), o_ret.astype(x.dtype)], axis=-1)
    return x + jnp.einsum('btc,cd->btd', cat, w_o)

def _ffn(x, g, w_gate_up, w_down):
    xn = _rmsnorm(x, g)
    a, b = jnp.split(jnp.einsum('btd,df->btf', xn, w_gate_up), 2, axis=-1)
    return x + jnp.einsum('btf,fd->btd', jax.nn.silu(a) * b, w_down)

def setup_inputs(seed: int = 0) -> dict:
    key = jax.random.key(seed)
    ks = jax.random.split(key, 16)
    f32 = jnp.float32
    kv_shape = (DEPTH, DEC_BATCH, WINDOW, SWA_KV_HEADS, SWA_HEAD_DIM)
    return {
        "x_prompt": jax.random.normal(ks[0], (BATCH, SEQ, D_MODEL), f32),
        "x_sample": jax.random.normal(ks[1], (DEC_BATCH, DEC_SEQ, D_MODEL), f32),
        "cache_k_win": jax.random.normal(ks[2], kv_shape, f32),
        "cache_v_win": jax.random.normal(ks[3], kv_shape, f32),
        "state_ret": 0.5 * jax.random.normal(ks[4], (DEPTH, DEC_BATCH, RET_HEADS, RET_KEY_DIM, RET_VAL_DIM), f32),
        "rel_bias": 0.5 * jax.random.normal(ks[5], (N_BUCKETS, SWA_HEADS), f32),
        "w_in": jax.random.normal(ks[6], (DEPTH, D_MODEL, IN_COLS), f32) * D_MODEL ** -0.5,
        "sinks": 0.5 * jax.random.normal(ks[7], (DEPTH, SWA_HEADS), f32),
        "w_o": jax.random.normal(ks[8], (DEPTH, MIX_WIDTH, D_MODEL), f32) * MIX_WIDTH ** -0.5,
        "norm_mix": 1.0 + 0.05 * jax.random.normal(ks[9], (DEPTH, D_MODEL), f32),
        "norm_ffn": 1.0 + 0.05 * jax.random.normal(ks[10], (DEPTH, D_MODEL), f32),
        "w_gate_up": jax.random.normal(ks[11], (DEPTH, D_MODEL, 2 * D_FF), f32) * D_MODEL ** -0.5,
        "w_down": jax.random.normal(ks[12], (DEPTH, D_FF, D_MODEL), f32) * D_FF ** -0.5,
        "norm_final": 1.0 + 0.05 * jax.random.normal(ks[13], (D_MODEL,), f32),
    }

def reference(x_prompt, x_sample, cache_k_win, cache_v_win, state_ret, rel_bias, w_in, sinks,
              w_o, norm_mix, norm_ffn, w_gate_up, w_down, norm_final):
    B, S, _ = x_prompt.shape
    DB, T, _ = x_sample.shape
    nblk = S // BLOCK
    pos_p = jnp.arange(S, dtype=jnp.int32)
    qpos_p = pos_p.reshape(nblk, BLOCK)
    kpos_p = jnp.concatenate([qpos_p - BLOCK, qpos_p], axis=1)
    pos_s = PAST_LEN + jnp.arange(T, dtype=jnp.int32)
    qpos_s = pos_s[None]
    kpos_s = jnp.concatenate([PAST_LEN - WINDOW + jnp.arange(WINDOW, dtype=jnp.int32), pos_s])[None]

    hp, hs = x_prompt, x_sample
    kp_new, vp_new, rp_new, ks_new, vs_new, rs_new = [], [], [], [], [], []
    for l in range(DEPTH):
        xn = _rmsnorm(hp, norm_mix[l])
        q_s, k_s, v_s, q_r, k_r, v_r, g_r = _project(xn, w_in[l], pos_p)
        kb = k_s.reshape(B, nblk, BLOCK, SWA_KV_HEADS, SWA_HEAD_DIM)
        vb = v_s.reshape(B, nblk, BLOCK, SWA_KV_HEADS, SWA_HEAD_DIM)
        k_band = jnp.concatenate([jnp.concatenate([jnp.zeros_like(kb[:, :1]), kb[:, :-1]], axis=1), kb], axis=2)
        v_band = jnp.concatenate([jnp.concatenate([jnp.zeros_like(vb[:, :1]), vb[:, :-1]], axis=1), vb], axis=2)
        o_swa = _swa_attend(q_s.reshape(B, nblk, BLOCK, SWA_HEADS, SWA_HEAD_DIM), k_band, v_band,
                            qpos_p, kpos_p, sinks[l], rel_bias).reshape(B, S, SWA_WIDTH)
        o_ret, st_p = _retention_prompt(q_r, k_r, v_r)
        hp = _mix_out(hp, o_swa, o_ret, g_r, w_o[l])
        hp = _ffn(hp, norm_ffn[l], w_gate_up[l], w_down[l])
        kp_new.append(k_s[:, S - WINDOW:])
        vp_new.append(v_s[:, S - WINDOW:])
        rp_new.append(st_p.astype(x_prompt.dtype))

        xn = _rmsnorm(hs, norm_mix[l])
        q_s, k_s, v_s, q_r, k_r, v_r, g_r = _project(xn, w_in[l], pos_s)
        k_all = jnp.concatenate([cache_k_win[l].astype(k_s.dtype), k_s], axis=1)
        v_all = jnp.concatenate([cache_v_win[l].astype(v_s.dtype), v_s], axis=1)
        o_swa = _swa_attend(q_s[:, None], k_all[:, None], v_all[:, None], qpos_s, kpos_s,
                            sinks[l], rel_bias).reshape(DB, T, SWA_WIDTH)
        st_s, o_ret = _retention_chunk(state_ret[l].astype(jnp.float32), q_r, k_r, v_r)
        hs = _mix_out(hs, o_swa, o_ret, g_r, w_o[l])
        hs = _ffn(hs, norm_ffn[l], w_gate_up[l], w_down[l])
        ks_new.append(k_all[:, -WINDOW:].astype(cache_k_win.dtype))
        vs_new.append(v_all[:, -WINDOW:].astype(cache_v_win.dtype))
        rs_new.append(st_s.astype(state_ret.dtype))

    y_prompt = _rmsnorm(hp, norm_final)
    y_sample = _rmsnorm(hs, norm_final)
    return (y_prompt, y_sample,
            jnp.stack(kp_new), jnp.stack(vp_new), jnp.stack(rp_new),
            jnp.stack(ks_new), jnp.stack(vs_new), jnp.stack(rs_new))


_drawn_inputs = setup_inputs


def setup_inputs(seed=0):
    import zlib

    import numpy as np

    out = dict(_drawn_inputs(seed))
    spreads = {}
    factors = {'sinks': 6.715}
    for name, (base, spread) in spreads.items():
        noise = np.random.default_rng([zlib.crc32(name.encode()), seed]).standard_normal(out[name].shape)
        drawn = base * np.exp(spread * noise) if base else spread * noise
        out[name] = __import__('jax').numpy.asarray(drawn.astype(out[name].dtype))
    for name, factor in factors.items():
        out[name] = (out[name] * factor).astype(out[name].dtype)
    return out
```

```python
from contextlib import ExitStack

import concourse.bass as bass
from concourse import mybir

F32 = mybir.dt.float32
F32R = mybir.dt.float32r
ACT = mybir.ActivationFunctionType
ALU = mybir.AluOpType
AX = mybir.AxisListType

P = 128
D_MODEL = 2048
DEPTH = 2
NP = 256
DB = 8
DT = 4
NS = DB * DT
T = NP + NS
KT = D_MODEL // P
D_FF = 5632
FT = D_FF // P
HEADS = 8
KV = 2
WIN = 128
RH = 4
EPS = 1e-6
SCALE = float(P) ** -0.5
KSCALE = float(256) ** -0.5
PAIR = 2 * P
IN_K, IN_V, IN_QR, IN_KR, IN_VR, IN_GR = 1024, 1280, 1536, 2560, 3584, 4608

R_IN, R_O, R_FFN, R_DOWN = 0, 22, 30, 74
ROUNDS = 98
P_IN, P_O, P_FFN, P_DOWN = 0, 22, 30, 74
PAIRS_PER_ACC = 41
FULL = (4, 4, 4, 4)
DOWN_ROUNDS = (FULL, FULL, (4, 4, 2, 2))
CREDIT = 2
LEAD = 3
XLEN = 3 * P

TABLES = {}
_at = 0
for _name, _n in (("ident", P), ("ones", P), ("eps", 1), ("gammaC", RH), ("kdecay", RH * 2),
                  ("head_rows", 64), ("cos", T), ("sin", T), ("decay", RH * NP), ("qdecay", RH * NS), ("decay_s", RH * NS),
                  ("kdecay_s", RH * DB), ("own", 4 * NS)):
    TABLES[_name] = (_at, _at + _n)
    _at += _n
TABLE_COLS = _at
FIRST_COLS = TABLES["cos"][0]

BANK_USES = {
    "pre": (("rms_mix", 4), ("k_tok", 7), ("v_tok", 5), ("v_tok_s", 7)),
    "group": (("s0", 4), ("kcT", 5), ("s1", 4), ("sampT", 6), ("pT0", 5), ("samp_s", 6), ("pT1", 5),
              ("pv0", 6), ("kr_tok", 7), ("kr_tok_s", 4), ("pv1", 6), ("samp_pT", 5), ("ret_s", 4),
              ("samp_pv", 6), ("o0", 7), ("vr_tok", 4), ("vr_tok_s", 5), ("o1", 6), ("ret_st", 4),
              ("st0", 5), ("st1", 4), ("st2", 5), ("st3", 4), ("st4", 5), ("st5", 4), ("st6", 5),
              ("st7", 4), ("gnorm", 5)),
    "post": (("rms_ffn", 4),),
}
BANK_OF = {n: b for uses in BANK_USES.values() for n, b in uses}


def _count(part, bank):
    return sum(1 for _, b in BANK_USES[part] if b == bank)


def use_number(name, layer, group=0):
    bank = BANK_OF[name]
    part = next(k for k, uses in BANK_USES.items() if name in dict(uses))
    names = [n for n, b in BANK_USES[part] if b == bank]
    pre, grp, post = (_count(k, bank) for k in ("pre", "group", "post"))
    at = layer * (pre + RH * grp + post) + names.index(name)
    if part == "group":
        return at + group * grp + pre
    if part == "post":
        return at + pre + RH * grp
    return at


def hybrid_trunk(nc, xT, cache_k, cache_v, state, rel_bias, w_in, sinks, sinksT, w_o, gainsT, w_gate_up,
                 w_down, tables, onehot, yT, new_kp, new_vp, new_rp, new_ks, new_vs, new_rs):
    bias_rows = nc.dram_tensor("bias_rows", (HEADS, P, XLEN), F32)

    with ExitStack() as ctx:
        def sb(name, shape, dt=F32):
            return ctx.enter_context(nc.sbuf_tensor(name, shape, dt))

        def sem(name):
            return ctx.enter_context(nc.semaphore(name))

        x_res = sb("x_res", [P, KT, T])
        xg_hi = sb("xg_hi", [P, KT, T], F32R)
        xg_lo = sb("xg_lo", [P, KT, T], F32R)
        raw = [sb(f"raw{s}", [P, 4, PAIR]) for s in range(4)]
        w_hi = [sb(f"w_hi{q}", [P, 2, PAIR], F32R) for q in range(4)]
        w_lo = [sb(f"w_lo{q}", [P, 2, PAIR], F32R) for q in range(4)]
        cst = sb("cst", [P, TABLE_COLS])
        gains = sb("gains", [P, 2 * DEPTH + 1, KT])
        sink_p = sb("sink_p", [P, DEPTH, HEADS])
        sink_s = sb("sink_s", [64, DEPTH])
        bias_s = sb("bias_s", [64, P + NS])
        rstd = sb("rstd", [P, T])
        sq_acc = sb("sq_acc", [P, T])
        pair_tmp = sb("pair_tmp", [P, 2, T])
        kT = sb("kT", [P, KV, T])
        v_tok = sb("v_tok", [P, 2, PAIR])
        v_tok_s = sb("v_tok_s", [NS, PAIR])
        rp_out = sb("rp_out", [P, 2, PAIR])
        kp_tok, ks_tok = rp_out[:, 0, :], rp_out[0:NS, 1, :]
        cat_hi = sb("cat_hi", [P, KT, T], F32R)
        cat_lo = sb("cat_lo", [P, KT, T], F32R)
        scratch0 = nc.sbuf_base
        hid_hi = sb("hid_hi", [P, FT - KT, T], F32R)
        hid_lo = sb("hid_lo", [P, FT - KT, T], F32R)
        scratch_end = nc.sbuf_base

        at = [scratch0]

        def over(name, shape, dt=F32):
            size = 4
            for n in shape[1:]:
                size *= n
            t = nc.alloc_sbuf_tensor_at(name, shape, dt, offset=at[0])
            at[0] += (size + 31) // 32 * 32
            assert at[0] <= scratch_end, (name, at[0] - scratch_end)
            return t

        qT = over("qT", [P, HEADS, T])
        biasT = over("biasT", [P, 2, NP])
        kc = over("kc", [P, 2, PAIR])
        vc = over("vc", [P, 2, PAIR])
        kcT = over("kcT", [P, 4, P])
        samp_sT = over("samp_sT", [P, 64])
        samp_p = over("samp_p", [64, P + NS])
        samp_pT = over("samp_pT", [P, 64])
        samp_pnT = over("samp_pnT", [NS, 64])
        samp_q = over("samp_q", [P, 64])
        k_rot = over("k_rot", [P, 2, T])
        q_rot = over("q_rot", [P, 2, T])
        vr = over("vr", [P, 2, T])
        rot_tmp = over("rot_tmp", [P, 2, T])
        gate = over("gate", [P, 2, T])
        kr_tok = over("kr_tok", [P, 2, PAIR])
        vr_tok = over("vr_tok", [P, 2, PAIR])
        kr_tok_s = over("kr_tok_s", [NS, PAIR])
        vr_tok_s = over("vr_tok_s", [NS, PAIR])
        k_own = over("k_own", [NS, 2, PAIR])
        ret_sT = over("ret_sT", [P, NP + P + NS])
        q_dec = over("q_dec", [P, 2, NS])
        q_head = over("q_head", [P, 2, NP])
        probs = [over(f"probs{h}", [P, NP + P]) for h in range(2)]
        pT = over("pT", [P, NP + P])
        stats = over("stats", [P, 24])
        setup_squares = nc.alloc_sbuf_tensor_at("setup_squares", [P, KT, T], F32, offset=scratch0)
        setup_hot = nc.alloc_sbuf_tensor_at("setup_hot", [33, XLEN + HEADS + DEPTH], F32, offset=at[0])
        setup_rows = nc.alloc_sbuf_tensor_at("setup_rows", [HEADS, XLEN + DEPTH], F32, offset=at[0] + 2048)
        st = over("st", [P, 2 * DB, PAIR])

        ps = ctx.enter_context(nc.psum_tensor("ps", [P, 8, 512], F32))
        acc = [ps[:, 0:2, 0:T], ps[:, 2:4, 0:T]]

        def bank(name, cols, parts=P, c0=0, p0=0):
            return ps[p0:p0 + parts, BANK_OF[name], c0:c0 + cols]

        def table(name, parts=P):
            a, b = TABLES[name]
            return cst[0:parts, a:b]

        ident, ones, eps, cos, sin = (table(n) for n in ("ident", "ones", "eps", "cos", "sin"))

        def over_pair(ap):
            return ap.unsqueeze(1).to_broadcast([P, 2, ap.shape[1]])

        setup_consts = sem("setup_consts")
        consts_loaded = sem("consts_loaded")
        gains_loaded = sem("gains_loaded")
        x_loaded = [sem(f"x_loaded{i}") for i in range(4)]
        raw_loaded = [sem(f"raw_loaded{s}") for s in range(4)]
        hi_ready = [sem(f"hi_ready{q}") for q in range(4)]
        split_ready = [sem(f"split_ready{q}") for q in range(4)]
        ring_used = [sem(f"ring_used{q}") for q in range(4)]
        acc_read = [sem(f"acc_read{a}") for a in range(2)]
        bank_filled = {b: sem(f"bank_filled{b}") for b in range(4, 8)}
        bank_read = {b: sem(f"bank_read{b}") for b in range(4, 8)}
        x_new = sem("x_new")
        xg_hi_ready = sem("xg_hi_ready")
        sq_ready = sem("sq_ready")
        sq_added = sem("sq_added")
        xg_ready = sem("xg_ready")
        std_ready = sem("std_ready")
        qkv_ready = sem("qkv_ready")
        q_staged = sem("q_staged")
        group_loaded = sem("group_loaded")
        group_used = sem("group_used")
        state_loaded = sem("state_loaded")
        state_stored = sem("state_stored")
        negmax_ready = sem("negmax_ready")
        exp_ready = sem("exp_ready")
        probs_ready = sem("probs_ready")
        samp_negmax = sem("samp_negmax")
        samp_exp = sem("samp_exp")
        samp_probs = sem("samp_probs")
        kr_ready = sem("kr_ready")
        qr_ready = sem("qr_ready")
        vr_ready = sem("vr_ready")
        own_ready = sem("own_ready")
        gate_raw = sem("gate_raw")
        gate_ready = sem("gate_ready")
        o_squared = sem("o_squared")
        ostd_ready = sem("ostd_ready")
        cat_hi_ready = sem("cat_hi_ready")
        mixed_ready = sem("mixed_ready")
        cat_ready = sem("cat_ready")
        rp_ready = sem("rp_ready")
        rp_stored = sem("rp_stored")
        rp_free = sem("rp_free")
        tok_left = sem("tok_left")
        mixer_left = sem("mixer_left")
        st_updated = sem("st_updated")
        tok_ready = sem("tok_ready")
        tok_stored = sem("tok_stored")
        ffn_gate = sem("ffn_gate")
        ffn_silu = sem("ffn_silu")
        hid_ready32 = sem("hid_ready32")
        hid_hi_ready = sem("hid_hi_ready")
        hid_ready = sem("hid_ready")
        down_done = sem("down_done")
        setup_done = sem("setup_done")
        setup_filled = sem("setup_filled")
        rows_ready = sem("rows_ready")
        rows_stored = sem("rows_stored")
        setup_loaded = sem("setup_loaded")
        bias_s_loaded = sem("bias_s_loaded")
        y_ready = sem("y_ready")
        out_stored = sem("out_stored")
        waited = sem("waited")

        def multiplied(e, r):
            e.wait_ge(ring_used[3], 2 * r + 3)

        def filled(e, name, layer, group=0):
            e.wait_ge(bank_filled[BANK_OF[name]], use_number(name, layer, group) + 1)

        def free(e, name, layer, group=0):
            e.wait_ge(bank_read[BANK_OF[name]], use_number(name, layer, group) + 1)

        def copied(e, name, layer, group=0):
            e.wait_ge(bank_read[BANK_OF[name]], use_number(name, layer, group) + 2)

        def steady(e):
            e.sem_inc(waited, 1)

        block = ctx.enter_context(nc.Block())

        def load_x(e, i):
            e.dma_start(x_res[:, 4 * i:4 * i + 4, :],
                        xT.rearrange("(t p) n -> p t n", p=P)[:, 4 * i:4 * i + 4, :]).then_inc(x_loaded[i], 16)

        @block.sync
        def _(sp):
            sp.dma_start(gains[:], gainsT).then_inc(gains_loaded, 16)
            load_x(sp, 0)

            def load_round(r, w, layer, col, kt0=0, sizes=FULL, chunks=4):
                view = w.rearrange("l (t p) n -> p l t n", p=P)
                kt = kt0
                for s in range(chunks):
                    j = 2 * s + 1
                    sp.wait_ge(split_ready[j % 4], 2 * r + j // 4 + 1)
                    src = view[:, bass.ds(layer, 1), kt:kt + sizes[s], bass.ds(col, PAIR)]
                    sp.dma_start(raw[s][:, 0:sizes[s], :],
                                 src.rearrange("p l t n -> p (l t) n")).then_inc(raw_loaded[s], 16)
                    kt += sizes[s]

            with sp.Fori(0, DEPTH) as layer:
                r0 = layer * ROUNDS
                for n, col in enumerate((IN_K, IN_V)):
                    load_round(r0 + n, w_in, layer, col)
                with sp.Fori(0, 4) as i:
                    load_round(r0 + 2 + i, w_in, layer, i * PAIR)
                with sp.Fori(0, RH) as g:
                    for n, col in enumerate((IN_KR, IN_QR, IN_VR, IN_GR)):
                        load_round(r0 + 6 + g * 4 + n, w_in, layer, g * PAIR + col)
                with sp.Fori(0, 8) as i:
                    load_round(r0 + R_O + i, w_o, layer, i * PAIR)
                with sp.Fori(0, FT // 2) as i:
                    load_round(r0 + R_FFN + i * 2, w_gate_up, layer, i * PAIR)
                    load_round(r0 + R_FFN + i * 2 + 1, w_gate_up, layer, i * PAIR + D_FF)
                with sp.Fori(0, 8) as i:
                    for n, sizes in enumerate(DOWN_ROUNDS):
                        load_round(r0 + R_DOWN + i * 3 + n, w_down, layer, i * PAIR, 16 * n, sizes)
            load_round(DEPTH * ROUNDS, w_in, 0, 0, chunks=2)

        @block.scalar
        def _(act):
            def split(r, j0, j1, sizes=FULL):
                for j in range(j0, j1):
                    s, q, n = j // 2, j % 4, sizes[j // 2] // 2
                    act.wait_ge(raw_loaded[s], r * 16 + 16)
                    act.wait_ge(ring_used[q], 2 * r + j // 4 + 1)
                    nc.scalar.activation(w_hi[q][:, 0:n, :], raw[s][:, n * (j % 2):n * (j % 2) + n, :],
                                         ACT.Copy).then_inc(hi_ready[q], 1)

            def split_on(r):
                split(r, LEAD, 8)
                split(r + 1, 0, LEAD)

            def pair_hi(t, norm):
                steady(act)
                for c in range(2):
                    ins = nc.scalar.activation(xg_hi[:, bass.ds(t + c, 1), :], x_res[:, bass.ds(t + c, 1), :],
                                               ACT.Copy, scale=gains[:, norm, bass.ds(t + c, 1)])
                ins.then_inc(xg_hi_ready, 1)

            def pair_squares(t, n):
                act.wait_ge(sq_added, n + 1)
                steady(act)
                nc.scalar.activation(pair_tmp[:], x_res[:, bass.ds(t, 2), :], ACT.Square).then_inc(sq_ready, 1)

            def residual_pair(t, norm, n):
                pair_hi(t, norm)
                pair_squares(t, n)

            def rms(name, layer):
                filled(act, name, layer)
                nc.scalar.activation(rstd[:], bank(name, T), ACT.Sqrt, bias=eps,
                                     scale=1.0 / D_MODEL).then_inc(bank_read[BANK_OF[name]], 1)

            def copy_out(dst, name, cols, parts=P, c0=0, done=True):
                ins = nc.scalar.activation(dst, bank(name, cols, parts, c0), ACT.Copy)
                if done:
                    ins.then_inc(bank_read[BANK_OF[name]], 1)
                return ins

            load_x(act, 1)
            act.dma_start(cst[:, 0:FIRST_COLS], tables[:, 0:FIRST_COLS]).then_inc(setup_consts, 16)
            load_x(act, 2)
            load_x(act, 3)
            act.dma_start(cst[:, FIRST_COLS:], tables[:, FIRST_COLS:]).then_inc(consts_loaded, 16)
            act.wait_ge(gains_loaded, 16)
            for i in range(4):
                act.wait_ge(x_loaded[i], 16)
                pair_hi(4 * i, 0)
                pair_hi(4 * i + 2, 0)
                if i < LEAD:
                    split(0, i, i + 1)
            for i in range(4):
                nc.scalar.activation(setup_squares[:, 4 * i:4 * i + 4, :], x_res[:, 4 * i:4 * i + 4, :],
                                     ACT.Square).then_inc(sq_ready, 2)
            act.wait_ge(setup_consts, 16)
            act.wait_ge(setup_filled, 1)
            nc.scalar.activation(setup_rows[:, 0:XLEN], ps[0:HEADS, 4, 0:XLEN], ACT.Copy).then_inc(bank_read[4], 1)
            nc.scalar.activation(sink_s[:], ps[0:64, 5, 0:DEPTH], ACT.Copy).then_inc(bank_read[5], 1)
            act.drain().then_inc(rows_ready, 1)

            with act.Fori(0, DEPTH) as layer:
                r0 = layer * ROUNDS
                split_on(r0)
                rms("rms_mix", layer)
                split(r0 + 1, LEAD, 7)
                act.wait_ge(rp_free, layer * RH + 1)
                filled(act, "k_tok", layer)
                copy_out(kp_tok, "k_tok", PAIR, done=False)
                copy_out(ks_tok, "k_tok", PAIR, NS, PAIR)
                act.drain().then_inc(tok_ready, 1)
                split(r0 + 1, 7, 8)
                split(r0 + 2, 0, 7)
                filled(act, "v_tok", layer)
                copy_out(v_tok[:], "v_tok", 512)
                split(r0 + 2, 7, 8)
                split(r0 + 3, 0, 1)
                filled(act, "v_tok_s", layer)
                copy_out(v_tok_s[:], "v_tok_s", PAIR, NS)
                act.drain().then_inc(tok_ready, 1)
                split(r0 + 3, 1, 8)
                split(r0 + 4, 0, 8)
                split(r0 + 5, 0, 8)
                split(r0 + 6, 0, LEAD)

                with act.Fori(0, RH) as g:
                    done = layer * RH + g
                    r = r0 + 6 + g * 4
                    split(r, 3, 5)
                    act.wait_ge(qkv_ready, layer * 6 + 6)
                    steady(act)
                    for h in range(2):
                        nc.scalar.activation(q_head[:, h:h + 1, :], qT[:, bass.ds(g + 4 * h, 1), 0:NP], ACT.Copy)
                    for h in range(2):
                        src = qT[:, 4 * h:4 * h + 4, bass.ds(g * 2 * DT + NP, 2 * DT)]
                        ins = nc.scalar.activation(
                            samp_q[:, 32 * h:32 * h + 32].rearrange("p (b h t) -> p b h t", b=2, h=4),
                            src.rearrange("p h (b t) -> p b h t", b=2), ACT.Copy)
                    ins.then_inc(q_staged, 1)
                    split(r, 5, 8)
                    split(r + 1, 0, 1)
                    filled(act, "kcT", layer, g)
                    copy_out(kcT[:], "kcT", 512)

                    def exponentials(h):
                        act.wait_ge(negmax_ready, done * 2 + h + 1)
                        s = stats[:, 12 * h:12 * h + 12]
                        nc.scalar.activation(probs[h][:, 0:P], probs[h][:, 0:P], ACT.Exp, bias=s[:, 2:3],
                                             accum_out=s[:, 4:5])
                        nc.scalar.activation(probs[h][:, P:P + NP], probs[h][:, P:P + NP], ACT.Exp,
                                             bias=s[:, 3:4], accum_out=s[:, 5:6])
                        nc.scalar.activation(s[:, 6:8], s[:, 2:4], ACT.Exp,
                                             bias=s[:, 10:11]).then_inc(exp_ready, 1)

                    exponentials(0)
                    split(r + 1, 1, 3)
                    filled(act, "sampT", layer, g)
                    copy_out(samp_sT[:], "sampT", 64)
                    split(r + 1, 3, 4)
                    exponentials(1)
                    split(r + 1, 4, 6)
                    filled(act, "pT0", layer, g)
                    copy_out(pT[:], "pT0", NP + P)
                    act.wait_ge(samp_negmax, done + 1)
                    nc.scalar.activation(samp_p[:], samp_p[:], ACT.Exp, bias=stats[0:64, 21:22],
                                         accum_out=stats[0:64, 22:23])
                    nc.scalar.activation(stats[0:64, 23:24], stats[0:64, 21:22], ACT.Exp,
                                         bias=sink_s[:, bass.ds(layer, 1)]).then_inc(samp_exp, 1)
                    split(r + 1, 6, 8)
                    split(r + 2, 0, 2)

                    def head_hi(h):
                        filled(act, f"pv{h}", layer, g)
                        steady(act)
                        copy_out(cat_hi[:, bass.ds(g + 4 * h, 1), 0:NP], f"pv{h}", NP,
                                 done=False).then_inc(cat_hi_ready, 1)

                    head_hi(0)
                    filled(act, "pT1", layer, g)
                    copy_out(pT[:], "pT1", NP + P)
                    split(r + 2, 2, 4)
                    filled(act, "kr_tok", layer, g)
                    steady(act)
                    for b in range(2):
                        ins = nc.scalar.activation(kr_tok[:, b, :], bank("kr_tok", PAIR, P, PAIR * b), ACT.Copy,
                                                   scale=table("kdecay")[:, bass.ds(g * 2 + b, 1)])
                    ins.then_inc(bank_read[BANK_OF["kr_tok"]], 1)
                    filled(act, "kr_tok_s", layer, g)
                    copy_out(kr_tok_s[:], "kr_tok_s", PAIR, NS)
                    split(r + 2, 4, 5)
                    head_hi(1)
                    split(r + 2, 5, 6)
                    filled(act, "samp_pT", layer, g)
                    copy_out(samp_pT[:], "samp_pT", 64, done=False)
                    copy_out(samp_pnT[:], "samp_pT", 64, NS, 64)
                    split(r + 2, 6, 8)
                    split(r + 3, 0, 2)
                    filled(act, "samp_pv", layer, g)
                    steady(act)
                    for h in range(2):
                        ins = nc.scalar.activation(
                            cat_hi[:, 4 * h:4 * h + 4, bass.ds(g * 2 * DT + NP, 2 * DT)].rearrange(
                                "p h (b t) -> p b h t", b=2),
                            bank("samp_pv", 32, P, 32 * h).rearrange("p (b h t) -> p b h t", b=2, h=4), ACT.Copy)
                    ins.then_inc(cat_hi_ready, 1)
                    split(r + 3, 2, 6)
                    filled(act, "vr_tok", layer, g)
                    copy_out(vr_tok[:], "vr_tok", 512)
                    filled(act, "vr_tok_s", layer, g)
                    copy_out(vr_tok_s[:], "vr_tok_s", PAIR, NS)
                    split(r + 3, 6, 8)
                    split(r + 4, 0, LEAD)
                    for v in range(2):
                        filled(act, f"o{v}", layer, g)
                        ins = nc.scalar.activation(rot_tmp[:, v, :], bank(f"o{v}", T), ACT.Square)
                    ins.then_inc(o_squared, 1)
                    filled(act, "ret_st", layer, g)
                    act.wait_ge(rp_free, done + 1)
                    act.wait_ge(tok_left, layer + 1)
                    copy_out(rp_out[:], "ret_st", 512)
                    act.drain().then_inc(rp_ready, 1)
                    act.wait_ge(gate_raw, done + 1)
                    nc.scalar.activation(gate[:], gate[:], ACT.Silu).then_inc(gate_ready, 1)
                    filled(act, "gnorm", layer, g)
                    nc.scalar.activation(rot_tmp[:, 0, :], bank("gnorm", T), ACT.Sqrt, bias=eps,
                                         scale=1.0 / PAIR).then_inc(bank_read[BANK_OF["gnorm"]], 1)
                    act.wait_ge(mixed_ready, done + 1)
                    steady(act)
                    nc.scalar.activation(cat_hi[:, bass.ds(g * 2 + HEADS, 2), :], vr[:],
                                         ACT.Copy).then_inc(cat_hi_ready, 1)

                with act.Fori(0, 4) as i:
                    for c in range(2):
                        split_on(r0 + R_O + i * 2 + c)
                        n = layer * 16 + i * 2 + c
                        act.wait_ge(x_new, n + 1)
                        residual_pair(i * 4 + 2 * c, layer * 2 + 1, n + 8)
                split_on(r0 + R_FFN)
                rms("rms_ffn", layer)
                act.wait_ge(mixer_left, layer + 1)
                steady(act)
                nc.scalar.preload_act_table(ACT.Silu)

                def gate_up(i, t_hi, first=False):
                    r = r0 + R_FFN + i * 2
                    n = layer * (FT // 2) + i
                    if not first:
                        split_on(r)
                    split(r + 1, LEAD, 4)
                    act.wait_ge(ffn_gate, n + 1)
                    nc.scalar.activation(pair_tmp[:], pair_tmp[:], ACT.Silu).then_inc(ffn_silu, 1)
                    split(r + 1, 4, 8)
                    split(r + 2, 0, LEAD)
                    act.wait_ge(hid_ready32, n + 1)
                    steady(act)
                    nc.scalar.activation(t_hi, pair_tmp[:], ACT.Copy).then_inc(hid_hi_ready, 1)

                gate_up(0, cat_hi[:, 0:2, :], first=True)
                with act.Fori(1, KT // 2) as i:
                    gate_up(i, cat_hi[:, bass.ds(i * 2, 2), :])
                with act.Fori(0, (FT - KT) // 2) as i:
                    gate_up(i + KT // 2, hid_hi[:, bass.ds(i * 2, 2), :])
                with act.Fori(0, 4) as i:
                    for c in range(2):
                        r = r0 + R_DOWN + i * 6 + 3 * c
                        split(r, LEAD, 8)
                        split(r + 1, 0, 8)
                        split(r + 2, 0, 8, DOWN_ROUNDS[2])
                        split(r + 3, 0, LEAD)
                        n = layer * 16 + 8 + i * 2 + c
                        act.wait_ge(x_new, n + 1)
                        residual_pair(i * 4 + 2 * c, layer * 2 + 2, n + 8)
            rms("rms_mix", DEPTH)
            for i in range(4):
                act.wait_ge(y_ready, 4 * i + 4)
                act.dma_start(yT.rearrange("(t p) n -> p t n", p=P)[:, 4 * i:4 * i + 4, :],
                              x_res[:, 4 * i:4 * i + 4, :]).then_inc(out_stored, 16)
            act.wait_ge(out_stored, 64)

        @block.vector
        def _(dve):
            def split(r, j0, j1, sizes=FULL):
                for j in range(j0, j1):
                    s, q, n = j // 2, j % 4, sizes[j // 2] // 2
                    dve.wait_ge(hi_ready[q], 2 * r + j // 4 + 1)
                    nc.vector.tensor_tensor(w_lo[q][:, 0:n, :], raw[s][:, n * (j % 2):n * (j % 2) + n, :],
                                            w_hi[q][:, 0:n, :].bitcast(F32),
                                            ALU.subtract).then_inc(split_ready[q], 1)

            def split_on(r):
                split(r, LEAD, 8)
                split(r + 1, 0, LEAD)

            def lo_of_pair(t, norm, n):
                dve.wait_ge(xg_hi_ready, n + 1)
                for c in range(2):
                    ins = nc.vector.scalar_tensor_tensor(
                        xg_lo[:, bass.ds(t + c, 1), :], x_res[:, bass.ds(t + c, 1), :],
                        gains[:, norm, bass.ds(t + c, 1)],
                        xg_hi[:, bass.ds(t + c, 1), :].bitcast(F32), ALU.mult, ALU.subtract)
                ins.then_inc(xg_ready, 1)

            def reciprocal_std(name, layer):
                copied(dve, name, layer)
                nc.vector.reciprocal(rstd[:], rstd[:])
                dve.drain()

            for q in range(4):
                dve.sem_inc(split_ready[q], CREDIT)
            for a in range(2):
                dve.sem_inc(acc_read[a], 1)
            for b in (6, 7):
                dve.sem_inc(bank_read[b], 1)
            dve.sem_inc(group_used, 1)
            nc.vector.memset(setup_hot[32:33, XLEN:XLEN + HEADS], 1.0).then_inc(setup_done, 1)
            dve.wait_ge(gains_loaded, 16)
            for i in range(4):
                lo_of_pair(4 * i, 0, 2 * i)
                lo_of_pair(4 * i + 2, 0, 2 * i + 1)
                if i < LEAD:
                    split(0, i, i + 1)
            dve.wait_ge(consts_loaded, 16)

            with dve.Fori(0, DEPTH) as layer:
                r0 = layer * ROUNDS
                split_on(r0)
                reciprocal_std("rms_mix", layer)

                def evacuate(dst, a, r):
                    multiplied(dve, r)
                    return nc.vector.tensor_tensor(dst, acc[a], over_pair(rstd[:]), ALU.mult)

                evacuate(kT[:], 0, r0).then_inc(acc_read[0], 1)
                dve.drain().then_inc(qkv_ready, 1)
                split_on(r0 + 1)
                evacuate(vr[:], 1, r0 + 1).then_inc(acc_read[1], 1)
                dve.drain().then_inc(qkv_ready, 1)
                for n in range(4):
                    split_on(r0 + 2 + n)
                    evacuate(qT[:, 2 * n:2 * n + 2, :], n % 2, r0 + 2 + n).then_inc(acc_read[n % 2], 1)
                    dve.drain().then_inc(qkv_ready, 1)

                with dve.Fori(0, RH) as g:
                    done = layer * RH + g
                    r = r0 + 6 + g * 4

                    def scores(h):
                        filled(dve, f"s{h}", layer, g)
                        if h == 0:
                            dve.wait_ge(group_loaded, done * 48 + 48)
                        s = stats[:, 12 * h:12 * h + 12]
                        nc.vector.tensor_copy(s[:, 10:11], sink_p[:, bass.ds(layer, 1), bass.ds(g + 4 * h, 1)])
                        nc.vector.scalar_tensor_tensor(probs[h][:, 0:P], bank(f"s{h}", P), SCALE,
                                                       biasT[:, h, P:NP], ALU.mult, ALU.add)
                        nc.vector.scalar_tensor_tensor(probs[h][:, P:P + NP], bank(f"s{h}", NP, P, P), SCALE,
                                                       biasT[:, h, :], ALU.mult,
                                                       ALU.add).then_inc(bank_read[BANK_OF[f"s{h}"]], 1)
                        dve.drain()
                        nc.vector.tensor_reduce(s[:, 0:1], probs[h][:, 0:P], AX.X, ALU.max)
                        nc.vector.tensor_reduce(s[:, 1:2], probs[h][:, P:P + NP], AX.X, ALU.max)
                        dve.drain()
                        nc.vector.tensor_scalar(s[:, 2:4], s[:, 0:2], s[:, 10:11], -1.0, ALU.max,
                                                ALU.mult).then_inc(negmax_ready, 1)

                    def normalise(h):
                        dve.wait_ge(exp_ready, done * 2 + h + 1)
                        s = stats[:, 12 * h:12 * h + 12]
                        nc.vector.tensor_tensor(s[:, 8:10], s[:, 4:6], s[:, 6:8], ALU.add)
                        dve.drain()
                        nc.vector.reciprocal(s[:, 0:2], s[:, 8:10])
                        dve.drain()
                        nc.vector.tensor_scalar(probs[h][:, 0:P], probs[h][:, 0:P], s[:, 0:1], None, ALU.mult)
                        nc.vector.tensor_scalar(probs[h][:, P:P + NP], probs[h][:, P:P + NP], s[:, 1:2], None,
                                                ALU.mult).then_inc(probs_ready, 1)

                    def rotate(x):
                        dve.drain()
                        nc.vector.tensor_tensor(rot_tmp[:], x[:], over_pair(cos), ALU.mult)
                        nc.vector.tensor_tensor(pair_tmp[:], x[:], over_pair(sin), ALU.mult)
                        dve.drain()
                        nc.vector.tensor_tensor(x[:, 0, :], rot_tmp[:, 0, :], pair_tmp[:, 1, :], ALU.subtract)
                        return nc.vector.tensor_tensor(x[:, 1, :], pair_tmp[:, 0, :], rot_tmp[:, 1, :], ALU.add)

                    def head_lo(h):
                        dve.wait_ge(cat_hi_ready, done * 4 + h + 1)
                        nc.vector.tensor_tensor(cat_lo[:, bass.ds(g + 4 * h, 1), 0:NP], bank(f"pv{h}", NP).unsqueeze(1),
                                                cat_hi[:, bass.ds(g + 4 * h, 1), 0:NP].bitcast(F32),
                                                ALU.subtract).then_inc(bank_read[BANK_OF[f"pv{h}"]], 1)

                    split(r, 3, 7)
                    scores(0)
                    split(r, 7, 8)
                    split(r + 1, 0, 2)
                    scores(1)
                    normalise(0)
                    split(r + 1, 2, 3)
                    multiplied(dve, r)
                    nc.vector.scalar_tensor_tensor(k_rot[:], acc[0], KSCALE, over_pair(rstd[:]), ALU.mult,
                                                   ALU.mult).then_inc(acc_read[0], 1)
                    rotate(k_rot).then_inc(kr_ready, 1)
                    split(r + 1, 3, 5)
                    normalise(1)
                    filled(dve, "samp_s", layer, g)
                    nc.vector.scalar_tensor_tensor(samp_p[:], bank("samp_s", P + NS, 64), SCALE, bias_s[:],
                                                   ALU.mult, ALU.add).then_inc(bank_read[BANK_OF["samp_s"]], 1)
                    dve.drain()
                    nc.vector.tensor_tensor(samp_p[:, P:P + NS], samp_p[:, P:P + NS],
                                            table("own", 64)[:, bass.ds(g * NS, NS)], ALU.add)
                    dve.drain()
                    nc.vector.tensor_reduce(stats[0:64, 20:21], samp_p[:], AX.X, ALU.max)
                    dve.drain()
                    nc.vector.tensor_scalar(stats[0:64, 21:22], stats[0:64, 20:21],
                                            sink_s[:, bass.ds(layer, 1)], -1.0, ALU.max,
                                            ALU.mult).then_inc(samp_negmax, 1)
                    split(r + 1, 5, 8)
                    dve.wait_ge(samp_exp, done + 1)
                    nc.vector.tensor_tensor(stats[0:64, 20:21], stats[0:64, 22:23], stats[0:64, 23:24], ALU.add)
                    dve.drain()
                    nc.vector.reciprocal(stats[0:64, 22:23], stats[0:64, 20:21])
                    dve.drain()
                    nc.vector.tensor_scalar(samp_p[:], samp_p[:], stats[0:64, 22:23], None,
                                            ALU.mult).then_inc(samp_probs, 1)
                    split(r + 2, 0, 3)
                    evacuate(q_rot[:], 1, r + 1).then_inc(acc_read[1], 1)
                    head_lo(0)
                    rotate(q_rot)
                    dve.drain()
                    nc.vector.tensor_tensor(
                        q_dec[:], q_rot[:, :, NP:T],
                        over_pair(table("qdecay")[:, bass.ds(g * NS, NS)]), ALU.mult).then_inc(qr_ready, 1)
                    split(r + 2, 3, 6)
                    head_lo(1)
                    split(r + 2, 6, 8)
                    split(r + 3, 0, 1)
                    filled(dve, "ret_s", layer, g)
                    nc.vector.tensor_tensor(ret_sT[:, 0:NP], bank("ret_s", NP),
                                            table("decay")[:, bass.ds(g * NP, NP)], ALU.mult)
                    nc.vector.tensor_tensor(ret_sT[:, NP:NP + P], bank("ret_s", P, P, NP),
                                            table("decay")[:, bass.ds(g * NP, P)], ALU.mult)
                    nc.vector.tensor_tensor(ret_sT[0:NS, NP + P:], bank("ret_s", NS, NS, NP + P),
                                            table("decay_s", NS)[:, bass.ds(g * NS, NS)],
                                            ALU.mult).then_inc(bank_read[BANK_OF["ret_s"]], 1)
                    split(r + 3, 1, 3)
                    evacuate(vr[:], 0, r + 2).then_inc(acc_read[0], 1)
                    dve.drain().then_inc(vr_ready, 1)
                    dve.wait_ge(cat_hi_ready, done * 4 + 3)
                    for h in range(2):
                        where = [x[:, 4 * h:4 * h + 4, bass.ds(g * 2 * DT + NP, 2 * DT)].rearrange(
                            "p h (b t) -> p b h t", b=2) for x in (cat_lo, cat_hi)]
                        ins = nc.vector.tensor_tensor(
                            where[0], bank("samp_pv", 32, P, 32 * h).rearrange("p (b h t) -> p b h t", b=2, h=4),
                            where[1].bitcast(F32), ALU.subtract)
                    ins.then_inc(bank_read[BANK_OF["samp_pv"]], 1)
                    dve.sem_inc(group_used, 1)
                    split(r + 3, 3, 8)

                    def own_keys(b):
                        nc.vector.tensor_scalar(k_own[:, b % 2, :], kr_tok_s[:],
                                                table("kdecay_s", NS)[:, bass.ds(g * DB + b, 1)], None,
                                                ALU.mult).then_inc(own_ready, 1)

                    split(r + 4, 0, LEAD)
                    copied(dve, "kr_tok_s", layer, g)
                    own_keys(0)
                    own_keys(1)
                    evacuate(gate[:], 1, r + 3).then_inc(acc_read[1], 1)
                    dve.drain().then_inc(gate_raw, 1)
                    dve.wait_ge(state_loaded, done * 32 + 32)
                    for b in range(DB):
                        filled(dve, f"st{b}", layer, g)
                        if b + 2 < DB:
                            own_keys(b + 2)
                        s = st[:, 2 * b:2 * b + 2, :]
                        nc.vector.scalar_tensor_tensor(
                            s, s, table("gammaC")[:, bass.ds(g, 1)],
                            bank(f"st{b}", 512).rearrange("p (k n) -> p k n", k=2), ALU.mult,
                            ALU.add).then_inc(bank_read[BANK_OF[f"st{b}"]], 1)
                    dve.drain().then_inc(st_updated, 1)
                    copied(dve, "gnorm", layer, g)
                    nc.vector.reciprocal(rot_tmp[:, 0, :], rot_tmp[:, 0, :])
                    dve.drain()
                    for v in range(2):
                        nc.vector.tensor_tensor(vr[:, v, :], bank(f"o{v}", T), rot_tmp[:, 0, :],
                                                ALU.mult).then_inc(bank_read[BANK_OF[f"o{v}"]], 1)
                    dve.drain()
                    dve.wait_ge(gate_ready, done + 1)
                    nc.vector.tensor_tensor(vr[:], vr[:], gate[:], ALU.mult).then_inc(mixed_ready, 1)
                    dve.wait_ge(cat_hi_ready, done * 4 + 4)
                    nc.vector.tensor_tensor(cat_lo[:, bass.ds(g * 2 + HEADS, 2), :], vr[:],
                                            cat_hi[:, bass.ds(g * 2 + HEADS, 2), :].bitcast(F32),
                                            ALU.subtract).then_inc(cat_ready, 1)

                def add_to_residual(a, r, i, c, n, norm):
                    multiplied(dve, r)
                    xs = x_res[:, bass.ds(i * 4 + 2 * c, 2), :]
                    nc.vector.tensor_tensor(xs, acc[a], xs, ALU.add).then_inc(acc_read[a], 1)
                    dve.drain().then_inc(x_new, 1)
                    lo_of_pair(i * 4 + 2 * c, norm, n)

                with dve.Fori(0, 4) as i:
                    for c in range(2):
                        split_on(r0 + R_O + i * 2 + c)
                        add_to_residual(c, r0 + R_O + i * 2 + c, i, c, layer * 16 + i * 2 + c + 8, layer * 2 + 1)

                split(r0 + R_FFN, LEAD, 8)
                split(r0 + R_FFN + 1, 0, LEAD)
                reciprocal_std("rms_ffn", layer)

                def gate_up(i, t_hi, t_lo, first=False):
                    r = r0 + R_FFN + i * 2
                    n = layer * (FT // 2) + i
                    if not first:
                        split_on(r)
                    evacuate(pair_tmp[:], 0, r).then_inc(acc_read[0], 1)
                    dve.drain().then_inc(ffn_gate, 1)
                    split(r + 1, 3, 6)
                    dve.wait_ge(ffn_silu, n + 1)
                    nc.vector.tensor_tensor(pair_tmp[:], pair_tmp[:], over_pair(rstd[:]), ALU.mult)
                    split(r + 1, 6, 8)
                    split(r + 2, 0, 3)
                    multiplied(dve, r + 1)
                    nc.vector.tensor_tensor(pair_tmp[:], acc[1], pair_tmp[:], ALU.mult).then_inc(acc_read[1], 1)
                    dve.drain().then_inc(hid_ready32, 1)
                    dve.wait_ge(hid_hi_ready, n + 1)
                    nc.vector.tensor_tensor(t_lo, pair_tmp[:], t_hi.bitcast(F32), ALU.subtract).then_inc(hid_ready, 1)

                gate_up(0, cat_hi[:, 0:2, :], cat_lo[:, 0:2, :], first=True)
                with dve.Fori(1, KT // 2) as i:
                    gate_up(i, cat_hi[:, bass.ds(i * 2, 2), :], cat_lo[:, bass.ds(i * 2, 2), :])
                with dve.Fori(0, (FT - KT) // 2) as i:
                    gate_up(i + KT // 2, hid_hi[:, bass.ds(i * 2, 2), :], hid_lo[:, bass.ds(i * 2, 2), :])

                with dve.Fori(0, 4) as i:
                    for c in range(2):
                        r = r0 + R_DOWN + i * 6 + 3 * c
                        split(r, LEAD, 8)
                        split(r + 1, 0, 8)
                        split(r + 2, 0, 8, DOWN_ROUNDS[2])
                        split(r + 3, 0, LEAD)
                        add_to_residual(c, r + 2, i, c, layer * 16 + 8 + i * 2 + c + 8, layer * 2 + 2)

            reciprocal_std("rms_mix", DEPTH)
            for t in range(KT):
                nc.vector.scalar_tensor_tensor(x_res[:, t, :], x_res[:, t, :], gains[:, 2 * DEPTH, t:t + 1],
                                               rstd[:], ALU.mult, ALU.mult).then_inc(y_ready, 1)

        @block.tensor
        def _(pe):
            def products(r, a, x_hi, x_lo, kt0=0, kt_x=0, j0=0, j1=8, sizes=FULL, kts=KT, ready=None,
                         beside=None):
                for j in range(j0, j1):
                    s, q, n = j // 2, j % 4, sizes[j // 2] // 2
                    k0 = kt0 + sum(sizes[0:s]) + n * (j % 2)
                    if ready is not None and j % 2 == 0:
                        ready(k0, sizes[s])
                    pe.wait_ge(split_ready[q], 2 * r + j // 4 + 1 + CREDIT)
                    for t in range(n):
                        k = k0 + t
                        x = k - kt0 + kt_x
                        for c in range(2):
                            cols = slice(P * c, P * c + P)
                            out = acc[a][:, c, :]
                            nc.tensor.matmul(out, w_hi[q][:, t, cols], x_hi[:, x, :], start=(k == 0),
                                             stop=False, skip_group_check=True)
                            nc.tensor.matmul(out, w_hi[q][:, t, cols], x_lo[:, x, :], start=False,
                                             stop=False, skip_group_check=True)
                            ins = nc.tensor.matmul(out, w_lo[q][:, t, cols], x_hi[:, x, :], start=False,
                                                   stop=(k == kts - 1), skip_group_check=True)
                            if t == n - 1 and c == 1:
                                ins.then_inc(ring_used[q], 1)
                            if beside is not None:
                                beside(4 * (j - j0) + 2 * t + c)

            def acc_free(a, layer, pair):
                pe.wait_ge(acc_read[a], layer * PAIRS_PER_ACC + pair + 1)

            def sum_partitions(name, layer, parts, group=0):
                free(pe, name, layer, group)
                for n, x in enumerate(parts):
                    ins = nc.tensor.matmul(bank(name, T), ones, x, start=(n == 0), stop=(n == len(parts) - 1))
                ins.then_inc(bank_filled[BANK_OF[name]], 1)

            for q in range(4):
                pe.sem_inc(ring_used[q], 1)
            pe.sem_inc(down_done, 1)
            pe.wait_ge(setup_done, 1)
            pe.wait_ge(setup_loaded, 48)
            pe.wait_ge(setup_consts, 16)
            nc.tensor.matmul(ps[0:HEADS, 4, 0:XLEN], setup_hot[:, XLEN:XLEN + HEADS], setup_hot[:, 0:XLEN],
                             start=True, stop=True)
            nc.tensor.matmul(ps[0:64, 5, 0:DEPTH], table("head_rows", HEADS), setup_rows[:, XLEN:XLEN + DEPTH],
                             start=True, stop=True).then_inc(setup_filled, 1)

            with pe.Fori(0, DEPTH) as layer:
                r0 = layer * ROUNDS

                def in_pair(r, a, n, j0=0, j1=8, first=False, beside=None):
                    def ready(k0, size):
                        pe.wait_ge(xg_ready, layer * 16 + (k0 + size) // 2)
                    if j0 == 0:
                        acc_free(a, layer, n)
                    products(r, a, xg_hi, xg_lo, j0=j0, j1=j1, ready=ready if first else None,
                             beside=beside)

                in_pair(r0, 0, 0, first=True)
                in_pair(r0 + 1, 1, 0, 0, 2)
                pe.wait_ge(sq_added, layer * 16 + 8 + 1)
                sum_partitions("rms_mix", layer, [sq_acc[:]])
                in_pair(r0 + 1, 1, 0, 2, 4)
                pe.wait_ge(qkv_ready, layer * 6 + 1)
                free(pe, "k_tok", layer)
                for kv in range(KV):
                    nc.tensor.transpose(bank("k_tok", P, P, P * kv), kT[:, kv, P:NP], ident)
                    ins = nc.tensor.transpose(bank("k_tok", P, NS, PAIR + P * kv), kT[:, kv, NP:T], ident)
                ins.then_inc(bank_filled[BANK_OF["k_tok"]], 1)
                in_pair(r0 + 1, 1, 0, 4, 8)
                in_pair(r0 + 2, 0, 1, 0, 4)
                pe.wait_ge(qkv_ready, layer * 6 + 2)
                free(pe, "v_tok", layer)
                for b in range(2):
                    for kv in range(KV):
                        ins = nc.tensor.transpose(bank("v_tok", P, P, PAIR * b + P * kv), vr[:, kv, P * b:P * b + P],
                                                  ident)
                ins.then_inc(bank_filled[BANK_OF["v_tok"]], 1)
                in_pair(r0 + 2, 0, 1, 4, 6)
                free(pe, "v_tok_s", layer)
                for kv in range(KV):
                    ins = nc.tensor.transpose(bank("v_tok_s", P, NS, P * kv), vr[:, kv, NP:T], ident)
                ins.then_inc(bank_filled[BANK_OF["v_tok_s"]], 1)
                in_pair(r0 + 2, 0, 1, 6, 8)
                for n in range(1, 4):
                    in_pair(r0 + 2 + n, n % 2, 1 + n // 2)

                with pe.Fori(0, RH) as g:
                    done = layer * RH + g
                    r = r0 + 6 + g * 4
                    pair = g * 2 + 3

                    def fill(name):
                        free(pe, name, layer, g)

                    def is_filled(ins, name):
                        ins.then_inc(bank_filled[BANK_OF[name]], 1)

                    def scores(h):
                        fill(f"s{h}")
                        nc.tensor.matmul(bank(f"s{h}", P), q_head[:, h, 0:P], kT[:, h, 0:P], start=True, stop=True)
                        is_filled(nc.tensor.matmul(bank(f"s{h}", NP, P, P), q_head[:, h, P:NP], kT[:, h, 0:NP],
                                                   start=True, stop=True), f"s{h}")

                    def transpose_probs(h):
                        pe.wait_ge(probs_ready, done * 2 + h + 1)
                        fill(f"pT{h}")
                        for b in range(3):
                            ins = nc.tensor.transpose(bank(f"pT{h}", P, P, P * b), probs[h][:, P * b:P * b + P], ident)
                        is_filled(ins, f"pT{h}")

                    def values(h):
                        copied(pe, f"pT{h}", layer, g)
                        fill(f"pv{h}")
                        v = [v_tok[:, b, P * h:P * h + P] for b in range(2)]
                        nc.tensor.matmul(bank(f"pv{h}", P), v[0], pT[:, 0:P], start=True, stop=True)
                        nc.tensor.matmul(bank(f"pv{h}", P, P, P), v[0], pT[:, P:NP], start=True, stop=False)
                        is_filled(nc.tensor.matmul(bank(f"pv{h}", P, P, P), v[1], pT[:, NP:NP + P], start=False,
                                                   stop=True), f"pv{h}")

                    in_pair(r, 0, pair, 0, 5)
                    pe.wait_ge(q_staged, done + 1)
                    scores(0)
                    in_pair(r, 0, pair, 5, 6)
                    pe.wait_ge(group_loaded, done * 48 + 48)
                    fill("kcT")
                    for b in range(2):
                        for kv in range(KV):
                            ins = nc.tensor.transpose(bank("kcT", P, P, PAIR * b + P * kv),
                                                      kc[:, b, P * kv:P * kv + P], ident)
                    is_filled(ins, "kcT")
                    in_pair(r, 0, pair, 6, 8)
                    scores(1)
                    in_pair(r + 1, 1, pair, 0, 1)
                    copied(pe, "kcT", layer, g)
                    fill("sampT")
                    for kv in range(KV):
                        for b in range(2):
                            c0 = 32 * kv + 16 * b
                            ins = nc.tensor.matmul(bank("sampT", 16, P, c0), kcT[:, 2 * b + kv, :],
                                                   samp_q[:, c0:c0 + 16], start=True, stop=True)
                    is_filled(ins, "sampT")
                    in_pair(r + 1, 1, pair, 1, 4)
                    transpose_probs(0)
                    copied(pe, "sampT", layer, g)
                    fill("samp_s")
                    steady(pe)
                    nc.tensor.transpose(bank("samp_s", P, 64), samp_sT[:], ident)
                    for kv in range(KV):
                        ins = nc.tensor.matmul(bank("samp_s", NS, 32, P, 32 * kv), samp_q[:, 32 * kv:32 * kv + 32],
                                               kT[:, kv, NP:T], start=True, stop=True)
                    is_filled(ins, "samp_s")
                    in_pair(r + 1, 1, pair, 4, 7)
                    values(0)
                    transpose_probs(1)
                    in_pair(r + 1, 1, pair, 7, 8)
                    in_pair(r + 2, 0, pair + 1, 0, 2)
                    pe.wait_ge(kr_ready, done + 1)
                    fill("kr_tok")
                    for b in range(2):
                        for d in range(2):
                            ins = nc.tensor.transpose(bank("kr_tok", P, P, PAIR * b + P * d),
                                                      k_rot[:, d, P * b:P * b + P], ident)
                    is_filled(ins, "kr_tok")
                    fill("kr_tok_s")
                    for d in range(2):
                        ins = nc.tensor.transpose(bank("kr_tok_s", P, NS, P * d), k_rot[:, d, NP:T], ident)
                    is_filled(ins, "kr_tok_s")
                    values(1)
                    in_pair(r + 2, 0, pair + 1, 2, 3)
                    pe.wait_ge(samp_probs, done + 1)
                    fill("samp_pT")
                    steady(pe)
                    nc.tensor.transpose(bank("samp_pT", 64), samp_p[:, 0:P], ident[0:64, 0:64])
                    is_filled(nc.tensor.transpose(bank("samp_pT", 64, NS, 64), samp_p[:, P:P + NS],
                                                  ident[0:64, 0:64]), "samp_pT")
                    in_pair(r + 2, 0, pair + 1, 3, 6)
                    pe.wait_ge(qr_ready, done + 1)
                    fill("ret_s")
                    for c0, n, m0, n0 in ((0, NP, 0, 0), (NP, P, P, P)):
                        for d in range(2):
                            nc.tensor.matmul(bank("ret_s", n, P, c0), k_rot[:, d, m0:m0 + P],
                                             q_rot[:, d, n0:n0 + n], start=(d == 0), stop=(d == 1))
                    for d in range(2):
                        ins = nc.tensor.matmul(bank("ret_s", NS, NS, NP + P), k_rot[:, d, NP:T], q_rot[:, d, NP:T],
                                               start=(d == 0), stop=(d == 1))
                    is_filled(ins, "ret_s")
                    in_pair(r + 2, 0, pair + 1, 6, 7)
                    copied(pe, "samp_pT", layer, g)
                    fill("samp_pv")
                    for kv in range(KV):
                        nc.tensor.matmul(bank("samp_pv", 32, P, 32 * kv), v_tok_s[:, P * kv:P * kv + P],
                                         samp_pnT[:, 32 * kv:32 * kv + 32], start=(kv == 0), stop=False,
                                         skip_group_check=True)
                        for b in range(2):
                            c0 = 32 * kv + 16 * b
                            ins = nc.tensor.matmul(bank("samp_pv", 16, P, c0), vc[:, b, P * kv:P * kv + P],
                                                   samp_pT[:, c0:c0 + 16], start=False, stop=True,
                                                   skip_group_check=True)
                    is_filled(ins, "samp_pv")
                    in_pair(r + 2, 0, pair + 1, 7, 8)

                    def state_times_q(v, n):
                        b, d = n // 2, n % 2
                        nc.tensor.matmul(bank(f"o{v}", DT, P, NP + DT * b), st[:, 2 * b + d, P * v:P * v + P],
                                         q_dec[:, d, DT * b:DT * b + DT], start=(n == 0), stop=False,
                                         skip_group_check=True)

                    pe.wait_ge(state_loaded, done * 32 + 32)
                    fill("o0")
                    in_pair(r + 3, 1, pair + 1, 0, 4, beside=lambda n: state_times_q(0, n))
                    pe.wait_ge(vr_ready, done + 1)
                    fill("vr_tok")
                    for b in range(2):
                        for d in range(2):
                            ins = nc.tensor.transpose(bank("vr_tok", P, P, PAIR * b + P * d),
                                                      vr[:, d, P * b:P * b + P], ident)
                    is_filled(ins, "vr_tok")
                    fill("vr_tok_s")
                    for d in range(2):
                        ins = nc.tensor.transpose(bank("vr_tok_s", P, NS, P * d), vr[:, d, NP:T], ident)
                    is_filled(ins, "vr_tok_s")
                    fill("o1")
                    in_pair(r + 3, 1, pair + 1, 4, 8, beside=lambda n: state_times_q(1, n))

                    copied(pe, "ret_s", layer, g)
                    copied(pe, "vr_tok", layer, g)
                    copied(pe, "vr_tok_s", layer, g)
                    for v in range(2):
                        dims = slice(P * v, P * v + P)
                        name = f"o{v}"
                        nc.tensor.matmul(bank(name, NP), vr_tok[:, 0, dims], ret_sT[:, 0:NP], start=False,
                                         stop=False, skip_group_check=True)
                        nc.tensor.matmul(bank(name, P, P, P), vr_tok[:, 1, dims], ret_sT[:, NP:NP + P],
                                         start=False, stop=False, skip_group_check=True)
                        is_filled(nc.tensor.matmul(bank(name, NS, P, NP), vr_tok_s[:, dims],
                                                   ret_sT[0:NS, NP + P:], start=False, stop=True,
                                                   skip_group_check=True), name)
                    fill("ret_st")
                    for d in range(2):
                        for b in range(2):
                            ins = nc.tensor.matmul(bank("ret_st", PAIR, P, PAIR * d), kr_tok[:, b, P * d:P * d + P],
                                                   vr_tok[:, b, :], start=(b == 0), stop=(b == 1))
                    is_filled(ins, "ret_st")
                    for b in range(DB):
                        pe.wait_ge(own_ready, done * DB + b + 1)
                        fill(f"st{b}")
                        for d in range(2):
                            ins = nc.tensor.matmul(bank(f"st{b}", PAIR, P, PAIR * d),
                                                   k_own[:, b % 2, P * d:P * d + P], vr_tok_s[:], start=True,
                                                   stop=True)
                        is_filled(ins, f"st{b}")
                    pe.wait_ge(o_squared, done + 1)
                    sum_partitions("gnorm", layer, [rot_tmp[:, v, :] for v in range(2)], g)

                copied(pe, "samp_pv", layer, RH - 1)
                pe.wait_ge(cat_ready, layer * RH + RH - 1)

                def cat_wait(k0, size):
                    if k0 + size == KT:
                        pe.wait_ge(cat_ready, layer * RH + RH)

                acc_free(0, layer, P_O // 2)
                products(r0 + R_O, 0, cat_hi, cat_lo, ready=cat_wait)
                acc_free(1, layer, P_O // 2)
                products(r0 + R_O + 1, 1, cat_hi, cat_lo)
                with pe.Fori(1, 4) as i:
                    for c in range(2):
                        acc_free(c, layer, i + P_O // 2)
                        products(r0 + R_O + i * 2 + c, c, cat_hi, cat_lo)

                def ffn_ready(k0, size):
                    pe.wait_ge(xg_ready, layer * 16 + 8 + (k0 + size) // 2)

                acc_free(0, layer, P_FFN // 2)
                products(r0 + R_FFN, 0, xg_hi, xg_lo, ready=ffn_ready)
                acc_free(1, layer, P_FFN // 2)
                products(r0 + R_FFN + 1, 1, xg_hi, xg_lo, j1=2)
                pe.wait_ge(sq_added, layer * 16 + 16 + 1)
                sum_partitions("rms_ffn", layer, [sq_acc[:]])
                products(r0 + R_FFN + 1, 1, xg_hi, xg_lo, j0=2)
                with pe.Fori(1, FT // 2) as i:
                    for c in range(2):
                        acc_free(c, layer, i + P_FFN // 2)
                        products(r0 + R_FFN + i * 2 + c, c, xg_hi, xg_lo)

                def hid_wait(k0, size):
                    pe.wait_ge(hid_ready, layer * (FT // 2) + (k0 + size) // 2)

                with pe.Fori(0, 4) as i:
                    for c in range(2):
                        acc_free(c, layer, i + P_DOWN // 2)
                        r = r0 + R_DOWN + i * 6 + 3 * c
                        products(r, c, cat_hi, cat_lo, kts=FT, ready=hid_wait)
                        products(r + 1, c, hid_hi, hid_lo, 16, 0, kts=FT, ready=hid_wait)
                        products(r + 2, c, hid_hi, hid_lo, 32, 16, sizes=DOWN_ROUNDS[2], kts=FT, ready=hid_wait)
                pe.sem_inc(down_done, 1)
            pe.wait_ge(sq_added, DEPTH * 16 + 8 + 1)
            sum_partitions("rms_mix", DEPTH, [sq_acc[:]])

        @block.gpsimd
        def _(pool):
            st_tiles = st[:].rearrange("p (b k) v -> p b k v", b=DB)

            def add_squares(n):
                pool.wait_ge(sq_ready, n + 1)
                nc.gpsimd.tensor_tensor(sq_acc[:], sq_acc[:], pair_tmp[:, 0, :], ALU.add)
                pool.drain()
                nc.gpsimd.tensor_tensor(sq_acc[:], sq_acc[:], pair_tmp[:, 1, :], ALU.add)
                pool.drain().then_inc(sq_added, 1)

            pool.dma_start(setup_hot[:, 0:XLEN], onehot).then_inc(setup_loaded, 16)
            pool.dma_start(setup_hot[0:32, XLEN:XLEN + HEADS], rel_bias).then_inc(setup_loaded, 16)
            with nc.allow_non_contiguous_dma(reason="16 sinks"):
                pool.dma_start(setup_rows[:, XLEN:XLEN + DEPTH], sinksT).then_inc(setup_loaded, 16)
            pool.dma_start(sink_p[:], sinks.rearrange("(o l) h -> o l h", o=1).to_broadcast([P, DEPTH, HEADS])
                           ).then_inc(bias_s_loaded, 16)
            pool.sem_inc(sq_added, 1)
            pool.sem_inc(rp_free, 1)
            first = setup_squares[:, 0:4, :]
            for i in range(1, 4):
                pool.wait_ge(sq_ready, 2 * i + 2)
                nc.gpsimd.tensor_tensor(first, first, setup_squares[:, 4 * i:4 * i + 4, :], ALU.add)
                pool.drain()
            nc.gpsimd.tensor_tensor(first[:, 0:2, :], first[:, 0:2, :], first[:, 2:4, :], ALU.add)
            pool.drain()
            nc.gpsimd.tensor_tensor(sq_acc[:], first[:, 0, :], first[:, 1, :], ALU.add)
            pool.drain().then_inc(sq_added, KT // 2)
            pool.wait_ge(rows_ready, 1)
            pool.dma_start(bass.AP(bias_rows, 0, [[P * XLEN, HEADS], [XLEN, P], [1, XLEN]]),
                           setup_rows[:, 0:XLEN].unsqueeze(1).to_broadcast([HEADS, P, XLEN])
                           ).then_inc(rows_stored, 16)
            pool.wait_ge(rows_stored, 16)

            def shifted(head, col, dims):
                return bass.AP(bias_rows, head * (P * XLEN) + (P - 1 + col), dims)

            for b in range(2):
                for h in range(HEADS):
                    row = (h // 4) * 32 + b * 16 + (h % 4) * DT
                    pool.dma_start(bias_s[row:row + DT, 0:P],
                                   shifted(h, 0, [[XLEN - 1, DT], [1, P]])).then_inc(bias_s_loaded, 16)
                    pool.dma_start(bias_s[row:row + DT, P:P + NS].rearrange("p (b t) -> p b t", b=DB),
                                   shifted(h, P, [[XLEN - 1, DT], [0, DB], [1, DT]])).then_inc(bias_s_loaded, 16)
            pool.wait_ge(bias_s_loaded, 16 + 2 * 2 * HEADS * 16)
            for w_new, w_old in ((new_ks, cache_k), (new_vs, cache_v)):
                pool.dma_start(w_new[:, :, 0:WIN - DT].rearrange("l b w k d -> (l b) (w k d)"),
                               w_old[:, :, DT:WIN].rearrange("l b w k d -> (l b) (w k d)")).then_inc(state_stored, 16)

            with pool.Fori(0, DEPTH) as layer:
                pool.wait_ge(down_done, layer + 1)
                pool.wait_ge(tok_ready, layer * 2 + 1)
                steady(pool)
                rows = new_ks[bass.ds(layer, 1)].rearrange("l b w k d -> (l b) w (k d)")
                vrows = new_vs[bass.ds(layer, 1)].rearrange("l b w k d -> (l b) w (k d)")
                pool.dma_start(new_kp[bass.ds(layer, 1)].rearrange("l o w k d -> (l o w) (k d)"),
                               kp_tok).then_inc(tok_stored, 16)
                for b in range(DB):
                    pool.dma_start(rows[b, WIN - DT:WIN, :], ks_tok[DT * b:DT * b + DT, :]).then_inc(tok_stored, 16)
                pool.wait_ge(tok_ready, layer * 2 + 2)
                steady(pool)
                pool.dma_start(new_vp[bass.ds(layer, 1)].rearrange("l o w k d -> (l o w) (k d)"),
                               v_tok[:, 1, :]).then_inc(tok_stored, 16)
                for b in range(DB):
                    pool.dma_start(vrows[b, WIN - DT:WIN, :], v_tok_s[DT * b:DT * b + DT, :]).then_inc(tok_stored, 16)

                pool.wait_ge(tok_stored, layer * 32 * (1 + DB) + 32 * (1 + DB))
                pool.sem_inc(tok_left, 1)

                with pool.Fori(0, RH) as g:
                    done = layer * RH + g

                    def head_rows(states, k):
                        return states[bass.ds(layer, 1), :, bass.ds(g, 1), P * k:P * k + P, :].rearrange(
                            "l b r p v -> p (l b r) v")

                    pool.wait_ge(group_used, done + 1)
                    steady(pool)
                    pool.dma_start(biasT[:], shifted(g, 0, [[XLEN - 1, P], [4 * P * XLEN, 2], [1, NP]])
                                   ).then_inc(group_loaded, 16)
                    for dst, src in ((kc, cache_k), (vc, cache_v)):
                        pool.dma_start(dst[:], src[bass.ds(layer, 1), bass.ds(g * 2, 2)].rearrange(
                            "l b w k d -> w (l b) (k d)")).then_inc(group_loaded, 16)
                    pool.wait_ge(state_stored, done * 32 + 32)
                    steady(pool)
                    for k in range(2):
                        pool.dma_start(st_tiles[:, :, k, :], head_rows(state, k)).then_inc(state_loaded, 16)
                    pool.wait_ge(rp_ready, done + 1)
                    steady(pool)
                    pool.dma_start(new_rp[bass.ds(layer, 1), :, bass.ds(g, 1)].rearrange(
                        "l o r (k p) v -> p (l o r k) v", p=P), rp_out[:]).then_inc(rp_stored, 16)
                    pool.wait_ge(rp_stored, done * 16 + 16)
                    pool.sem_inc(rp_free, 1)
                    pool.wait_ge(st_updated, done + 1)
                    steady(pool)
                    for k in range(2):
                        pool.dma_start(head_rows(new_rs, k), st_tiles[:, :, k, :]).then_inc(state_stored, 16)

                pool.wait_ge(state_stored, layer * RH * 32 + RH * 32 + 32)
                pool.sem_inc(mixer_left, 1)
                for part in range(2):
                    if part == 0:
                        copied(pool, "rms_mix", layer)
                    else:
                        copied(pool, "rms_ffn", layer)
                    steady(pool)
                    nc.gpsimd.memset(sq_acc[:], 0.0)
                    pool.drain()
                    with pool.Fori(0, KT // 2) as i:
                        add_squares(layer * 16 + 8 * part + 8 + i)


def shape_tables():
    import numpy as np

    f = np.float32
    cst = np.zeros((P, TABLE_COLS), f)

    def put(name, value, parts=P):
        a, b = TABLES[name]
        cst[0:parts, a:b] = np.asarray(value, np.float64).reshape(-1, b - a) if np.ndim(value) else value

    put("ident", np.eye(P))
    put("ones", 1.0)
    put("eps", EPS)
    gamma = 1.0 - 2.0 ** (-5.0 - np.arange(RH))
    put("gammaC", gamma ** DT)
    tok = np.arange(P)
    put("kdecay", np.stack([gamma[h] ** (NP - 1.0 - (tok + P * b)) for h in range(RH) for b in range(2)], 1))
    inv = f(1.0) / (f(10000.0) ** np.linspace(0.0, 1.0, P, dtype=f)).astype(f)
    pos = np.concatenate([np.arange(NP), np.tile(2048 + np.arange(DT), DB)]).astype(f)
    angle = (pos[None, :] * inv[:, None]).astype(f).astype(np.float64)
    put("cos", np.cos(angle))
    put("sin", np.sin(angle))
    n = np.arange(NP)[None, :] - tok[:, None]
    put("decay", np.concatenate([np.where(n >= 0, gamma[h] ** np.maximum(n, 0), 0.0) for h in range(RH)], 1))
    row = np.arange(NS)
    put("qdecay", np.concatenate([gamma[h] ** (row % DT + 1.0) for h in range(RH)]))
    n = row[None, :] - row[:, None]
    same = row[None, :] // DT == row[:, None] // DT
    put("decay_s", np.concatenate([np.where(same & (n >= 0), gamma[h] ** np.maximum(n, 0), 0.0)
                                   for h in range(RH)], 1), NS)
    put("kdecay_s", np.stack([np.where(row // DT == b, gamma[h] ** (DT - 1.0 - row % DT), 0.0)
                              for h in range(RH) for b in range(DB)], 1), NS)
    batch = (np.arange(64) // 16) % 2
    put("own", np.concatenate([np.where(row[None, :] // DT == 2 * g + batch[:, None], 0.0, -1e30)
                               for g in range(4)], 1), 64)
    rows_head = (np.arange(64) // 32) * 4 + (np.arange(64) % 16) // DT
    put("head_rows", np.arange(HEADS)[:, None] == rows_head[None, :], HEADS)

    delta = NP - 1 - np.arange(XLEN)
    d = np.maximum(delta, 1).astype(f)
    large = 16 + (np.log(d / f(16)).astype(f) / f(np.log(8.0)) * f(16)).astype(np.int32)
    bucket = np.where(delta < 16, np.maximum(delta, 0), np.minimum(large, 31))
    valid = (delta >= 0) & (delta < WIN)
    hot = np.zeros((33, XLEN), f)
    hot[bucket[valid], np.nonzero(valid)[0]] = 1.0
    hot[32, ~valid] = -1e30
    return cst, hot


def kernel(x_prompt, x_sample, cache_k_win, cache_v_win, state_ret, rel_bias, w_in, sinks, w_o, norm_mix,
           norm_ffn, w_gate_up, w_down, norm_final):
    import numpy as np
    import concourse.bacc as bacc
    from concourse.bass_utils import run_bass_kernel_spmd

    cst, hot = shape_tables()
    x = np.concatenate([np.asarray(x_prompt).reshape(NP, D_MODEL), np.asarray(x_sample).reshape(NS, D_MODEL)])
    gains = np.stack([g for l in range(DEPTH) for g in (np.asarray(norm_mix)[l], np.asarray(norm_ffn)[l])]
                     + [np.asarray(norm_final)])
    ins = {
        "xT": x.T, "cache_k": cache_k_win, "cache_v": cache_v_win, "state": state_ret, "rel_bias": rel_bias,
        "w_in": w_in, "sinks": sinks, "sinksT": np.asarray(sinks).T, "w_o": w_o,
        "gainsT": gains.reshape(2 * DEPTH + 1, KT, P).transpose(2, 0, 1), "w_gate_up": w_gate_up,
        "w_down": w_down, "tables": cst, "onehot": hot,
    }
    ins = {k: np.ascontiguousarray(v) for k, v in ins.items()}
    outs = {
        "yT": (D_MODEL, T), "new_kp": (DEPTH, 1, WIN, KV, P), "new_vp": (DEPTH, 1, WIN, KV, P),
        "new_rp": (DEPTH, 1, RH, PAIR, PAIR), "new_ks": (DEPTH, DB, WIN, KV, P), "new_vs": (DEPTH, DB, WIN, KV, P),
        "new_rs": (DEPTH, DB, RH, PAIR, PAIR),
    }
    nc = bacc.Bacc("TRN2", target_bir_lowering=False, num_devices=1)
    aps = [nc.dram_tensor(k, v.shape, mybir.dt.from_np(v.dtype), kind="ExternalInput").ap() for k, v in ins.items()]
    aps += [nc.dram_tensor(k, shape, F32, kind="ExternalOutput").ap() for k, shape in outs.items()]
    hybrid_trunk(nc, *aps)
    r = run_bass_kernel_spmd(nc, [ins], core_ids=[0]).results[0]
    y = np.ascontiguousarray(r["yT"].T)
    return (y[0:NP].reshape(1, NP, D_MODEL), y[NP:T].reshape(DB, DT, D_MODEL), r["new_kp"], r["new_vp"],
            r["new_rp"], r["new_ks"], r["new_vs"], r["new_rs"])
```

```python
from contextlib import ExitStack

import concourse.bass as bass
from concourse import mybir

F32 = mybir.dt.float32
F32R = mybir.dt.float32r
ACT = mybir.ActivationFunctionType
ALU = mybir.AluOpType
AX = mybir.AxisListType

P = 128
D_MODEL = 2048
DEPTH = 2
NP = 256
DB = 8
DT = 4
NS = DB * DT
T = NP + NS
KT = D_MODEL // P
D_FF = 5632
FT = D_FF // P
HEADS = 8
KV = 2
WIN = 128
RH = 4
EPS = 1e-6
SCALE = float(P) ** -0.5
KSCALE = float(256) ** -0.5
PAIR = 2 * P
IN_K, IN_V, IN_QR, IN_KR, IN_VR, IN_GR = 1024, 1280, 1536, 2560, 3584, 4608
COPIES = P // NS

R_IN, R_O, R_FFN, R_DOWN = 0, 22, 30, 74
ROUNDS = 98
P_IN, P_O, P_FFN, P_DOWN = 0, 22, 30, 74
PAIRS_PER_ACC = 41
FULL = (4, 4, 4, 4)
DOWN_ROUNDS = (FULL, FULL, (4, 4, 2, 2))
CREDIT = 2
LEAD = 3
GLEAD = 6
OWN = 4
XLEN = 3 * P

TABLES = {}
_at = 0
for _name, _n in (("ident", P), ("ones", P), ("eps", 1), ("gammaC", RH), ("kdecay", RH * 2),
                  ("head_rows", 64), ("cos", T), ("sin", T), ("decay", RH * NP), ("qdecay", RH * NS), ("decay_s", RH * NS),
                  ("kdecay_s", RH), ("own_rows", DB), ("own", 4 * NS)):
    TABLES[_name] = (_at, _at + _n)
    _at += _n
TABLE_COLS = _at
FIRST_COLS = TABLES["cos"][0]

BANK_USES = {
    "pre": (("rms_mix", 4), ("k_tok", 7), ("v_tok", 5), ("v_tok_s", 7)),
    "group": (("s0", 4), ("kcT", 5), ("s1", 4), ("sampT", 6), ("pT0", 5), ("samp_s", 6), ("pT1", 5),
              ("pv0", 6), ("pv1", 7), ("samp_pT", 5), ("o0", 6), ("samp_pv", 4), ("o1", 7), ("kr_tok", 5),
              ("kr_copies", 4), ("ret_s", 5), ("vr_tok", 4), ("vr_copies", 5), ("ret_st", 4),
              ("st0", 5), ("st1", 4), ("st2", 5), ("st3", 4), ("st4", 5), ("st5", 4), ("st6", 5),
              ("st7", 4), ("gnorm", 5)),
    "post": (("rms_ffn", 4),),
}
BANK_OF = {n: b for uses in BANK_USES.values() for n, b in uses}


def _count(part, bank):
    return sum(1 for _, b in BANK_USES[part] if b == bank)


def use_number(name, layer, group=0):
    bank = BANK_OF[name]
    part = next(k for k, uses in BANK_USES.items() if name in dict(uses))
    names = [n for n, b in BANK_USES[part] if b == bank]
    pre, grp, post = (_count(k, bank) for k in ("pre", "group", "post"))
    at = layer * (pre + RH * grp + post) + names.index(name)
    if part == "group":
        return at + group * grp + pre
    if part == "post":
        return at + pre + RH * grp
    return at


def hybrid_trunk(nc, xT, cache_k, cache_v, state, rel_bias, w_in, sinks, sinksT, w_o, gainsT, w_gate_up,
                 w_down, tables, onehot, yT, new_kp, new_vp, new_rp, new_ks, new_vs, new_rs):
    bias_rows = nc.dram_tensor("bias_rows", (HEADS, P, XLEN), F32)

    with ExitStack() as ctx:
        def sb(name, shape, dt=F32):
            return ctx.enter_context(nc.sbuf_tensor(name, shape, dt))

        def sem(name):
            return ctx.enter_context(nc.semaphore(name))

        x_res = sb("x_res", [P, KT, T])
        xg_hi = sb("xg_hi", [P, KT, T], F32R)
        xg_lo = sb("xg_lo", [P, KT, T], F32R)
        raw = [sb(f"raw{s}", [P, 4, PAIR]) for s in range(4)]
        w_hi = [sb(f"w_hi{q}", [P, 2, PAIR], F32R) for q in range(4)]
        w_lo = [sb(f"w_lo{q}", [P, 2, PAIR], F32R) for q in range(4)]
        cst = sb("cst", [P, TABLE_COLS])
        gains = sb("gains", [P, 2 * DEPTH + 1, KT])
        sink_p = sb("sink_p", [P, DEPTH, HEADS])
        sink_s = sb("sink_s", [64, DEPTH])
        bias_s = sb("bias_s", [64, P + NS])
        rstd = sb("rstd", [P, T])
        sq_acc = sb("sq_acc", [P, T])
        pair_tmp = sb("pair_tmp", [P, 2, T])
        kT = sb("kT", [P, KV, T])
        v_tok = sb("v_tok", [P, 2, PAIR])
        v_tok_s = sb("v_tok_s", [NS, PAIR])
        rp_out = sb("rp_out", [P, 2, PAIR])
        kp_tok, ks_tok = rp_out[:, 0, :], rp_out[0:NS, 1, :]
        cat_hi = sb("cat_hi", [P, KT, T], F32R)
        cat_lo = sb("cat_lo", [P, KT, T], F32R)
        scratch0 = nc.sbuf_base
        hid_hi = sb("hid_hi", [P, FT - KT, T], F32R)
        hid_lo = sb("hid_lo", [P, FT - KT, T], F32R)
        scratch_end = nc.sbuf_base

        at = [scratch0]

        def over(name, shape, dt=F32):
            size = 4
            for n in shape[1:]:
                size *= n
            t = nc.alloc_sbuf_tensor_at(name, shape, dt, offset=at[0])
            at[0] += (size + 31) // 32 * 32
            assert at[0] <= scratch_end, (name, at[0] - scratch_end)
            return t

        qT = over("qT", [P, HEADS, T])
        biasT = over("biasT", [P, 2, NP])
        kc = over("kc", [P, 2, PAIR])
        vc = over("vc", [P, 2, PAIR])
        samp_sT = over("samp_sT", [P, 64])
        samp_p = over("samp_p", [64, P + NS])
        samp_pT = over("samp_pT", [P, 64])
        samp_pnT = over("samp_pnT", [NS, 64])
        samp_q = over("samp_q", [P, 64])
        k_rot = over("k_rot", [P, 2, T])
        q_rot = over("q_rot", [P, 2, T])
        vr = over("vr", [P, 2, T])
        rot_tmp = over("rot_tmp", [P, 2, T])
        k_copies = nc.alloc_sbuf_tensor_at("k_copies", [P, 2, P], F32, offset=at[0])
        v_copies = nc.alloc_sbuf_tensor_at("v_copies", [P, 2, P], F32, offset=at[0] + 2 * P * 4)
        gate = over("gate", [P, 2, T])
        kr_tok = over("kr_tok", [P, 2, PAIR])
        vr_tok = over("vr_tok", [P, 2, PAIR])
        vr_tok_s = over("vr_tok_s", [NS, PAIR])
        k_stack = over("k_stack", [P, PAIR], F32R)
        v_stack = over("v_stack", [P, PAIR], F32R)
        pT = nc.alloc_sbuf_tensor_at("pT", [P, NP + P], F32, offset=at[0])
        ret_sT = over("ret_sT", [P, NP + P + NS])
        cos_std = over("cos_std", [P, T])
        sin_std = over("sin_std", [P, T])
        q_dec = over("q_dec", [P, 2, NS])
        k_own = nc.alloc_sbuf_tensor_at("k_own", [P, OWN, PAIR], F32R, offset=at[0])
        q_head = over("q_head", [P, 2, NP])
        kcT = over("kcT", [P, 4, P])
        probs = [over(f"probs{h}", [P, NP + P]) for h in range(2)]
        stats = over("stats", [P, 24])
        setup_squares = nc.alloc_sbuf_tensor_at("setup_squares", [P, KT, T], F32, offset=scratch0)
        setup_hot = nc.alloc_sbuf_tensor_at("setup_hot", [33, XLEN + HEADS + DEPTH], F32, offset=at[0])
        setup_rows = nc.alloc_sbuf_tensor_at("setup_rows", [HEADS, XLEN + DEPTH], F32, offset=at[0] + 2048)
        st = over("st", [P, 2 * DB, PAIR])

        ps = ctx.enter_context(nc.psum_tensor("ps", [P, 8, 512], F32))
        acc = [ps[:, 0:2, 0:T], ps[:, 2:4, 0:T]]

        def bank(name, cols, parts=P, c0=0, p0=0):
            return ps[p0:p0 + parts, BANK_OF[name], c0:c0 + cols]

        def table(name, parts=P):
            a, b = TABLES[name]
            return cst[0:parts, a:b]

        ident, ones, eps, cos, sin = (table(n) for n in ("ident", "ones", "eps", "cos", "sin"))

        def over_pair(ap):
            return ap.unsqueeze(1).to_broadcast([P, 2, ap.shape[1]])

        setup_consts = sem("setup_consts")
        consts_loaded = sem("consts_loaded")
        gains_loaded = sem("gains_loaded")
        x_loaded = [sem(f"x_loaded{i}") for i in range(4)]
        raw_loaded = [sem(f"raw_loaded{s}") for s in range(4)]
        hi_ready = [sem(f"hi_ready{q}") for q in range(4)]
        split_ready = [sem(f"split_ready{q}") for q in range(4)]
        ring_used = [sem(f"ring_used{q}") for q in range(4)]
        acc_read = [sem(f"acc_read{a}") for a in range(2)]
        bank_filled = {b: sem(f"bank_filled{b}") for b in range(4, 8)}
        bank_read = {b: sem(f"bank_read{b}") for b in range(4, 8)}
        x_new = sem("x_new")
        xg_hi_ready = sem("xg_hi_ready")
        sq_ready = sem("sq_ready")
        sq_added = sem("sq_added")
        xg_ready = sem("xg_ready")
        qkv_ready = sem("qkv_ready")
        q_staged = sem("q_staged")
        group_loaded = sem("group_loaded")
        group_used = sem("group_used")
        state_loaded = sem("state_loaded")
        state_stored = sem("state_stored")
        negmax_ready = sem("negmax_ready")
        exp_ready = sem("exp_ready")
        sum_inverted = sem("sum_inverted")
        probs_ready = sem("probs_ready")
        samp_negmax = sem("samp_negmax")
        samp_exp = sem("samp_exp")
        samp_probs = sem("samp_probs")
        kr_ready = sem("kr_ready")
        qr_ready = sem("qr_ready")
        vr_ready = sem("vr_ready")
        k_stacked = sem("k_stacked")
        v_stacked = sem("v_stacked")
        k_hi_ready = sem("k_hi_ready")
        v_hi_ready = sem("v_hi_ready")
        own_ready = sem("own_ready")
        gate_raw = sem("gate_raw")
        gate_ready = sem("gate_ready")
        o_squared = sem("o_squared")
        cat_hi_ready = sem("cat_hi_ready")
        mixed_ready = sem("mixed_ready")
        cat_ready = sem("cat_ready")
        rp_ready = sem("rp_ready")
        rp_stored = sem("rp_stored")
        rp_free = sem("rp_free")
        tok_left = sem("tok_left")
        mixer_left = sem("mixer_left")
        st_updated = sem("st_updated")
        tok_ready = sem("tok_ready")
        tok_stored = sem("tok_stored")
        ffn_gate = sem("ffn_gate")
        ffn_silu = sem("ffn_silu")
        hid_ready32 = sem("hid_ready32")
        hid_hi_ready = sem("hid_hi_ready")
        hid_ready = sem("hid_ready")
        down_done = sem("down_done")
        setup_done = sem("setup_done")
        setup_filled = sem("setup_filled")
        rows_ready = sem("rows_ready")
        rows_stored = sem("rows_stored")
        setup_loaded = sem("setup_loaded")
        bias_s_loaded = sem("bias_s_loaded")
        y_ready = sem("y_ready")
        out_stored = sem("out_stored")
        waited = sem("waited")

        def multiplied(e, r):
            e.wait_ge(ring_used[3], 2 * r + 3)

        def filled(e, name, layer, group=0):
            e.wait_ge(bank_filled[BANK_OF[name]], use_number(name, layer, group) + 1)

        def free(e, name, layer, group=0):
            e.wait_ge(bank_read[BANK_OF[name]], use_number(name, layer, group) + 1)

        def copied(e, name, layer, group=0):
            e.wait_ge(bank_read[BANK_OF[name]], use_number(name, layer, group) + 2)

        def steady(e):
            e.sem_inc(waited, 1)

        block = ctx.enter_context(nc.Block())

        def load_x(e, i):
            e.dma_start(x_res[:, 4 * i:4 * i + 4, :],
                        xT.rearrange("(t p) n -> p t n", p=P)[:, 4 * i:4 * i + 4, :]).then_inc(x_loaded[i], 16)

        @block.sync
        def _(sp):
            sp.dma_start(gains[:], gainsT).then_inc(gains_loaded, 16)
            load_x(sp, 0)

            def load_round(r, w, layer, col, kt0=0, sizes=FULL, chunks=4):
                view = w.rearrange("l (t p) n -> p l t n", p=P)
                kt = kt0
                for s in range(chunks):
                    j = 2 * s + 1
                    sp.wait_ge(split_ready[j % 4], 2 * r + j // 4 + 1)
                    src = view[:, bass.ds(layer, 1), kt:kt + sizes[s], bass.ds(col, PAIR)]
                    sp.dma_start(raw[s][:, 0:sizes[s], :],
                                 src.rearrange("p l t n -> p (l t) n")).then_inc(raw_loaded[s], 16)
                    kt += sizes[s]

            with sp.Fori(0, DEPTH) as layer:
                r0 = layer * ROUNDS
                for n, col in enumerate((IN_K, IN_V)):
                    load_round(r0 + n, w_in, layer, col)
                with sp.Fori(0, 4) as i:
                    load_round(r0 + 2 + i, w_in, layer, i * PAIR)
                with sp.Fori(0, RH) as g:
                    for n, col in enumerate((IN_QR, IN_KR, IN_VR, IN_GR)):
                        load_round(r0 + 6 + g * 4 + n, w_in, layer, g * PAIR + col)
                with sp.Fori(0, 8) as i:
                    load_round(r0 + R_O + i, w_o, layer, i * PAIR)
                with sp.Fori(0, FT // 2) as i:
                    load_round(r0 + R_FFN + i * 2, w_gate_up, layer, i * PAIR)
                    load_round(r0 + R_FFN + i * 2 + 1, w_gate_up, layer, i * PAIR + D_FF)
                with sp.Fori(0, 8) as i:
                    for n, sizes in enumerate(DOWN_ROUNDS):
                        load_round(r0 + R_DOWN + i * 3 + n, w_down, layer, i * PAIR, 16 * n, sizes)
            load_round(DEPTH * ROUNDS, w_in, 0, 0, chunks=2)

        @block.scalar
        def _(act):
            def split(r, j0, j1, sizes=FULL):
                for j in range(j0, j1):
                    s, q, n = j // 2, j % 4, sizes[j // 2] // 2
                    act.wait_ge(raw_loaded[s], r * 16 + 16)
                    act.wait_ge(ring_used[q], 2 * r + j // 4 + 1)
                    nc.scalar.activation(w_hi[q][:, 0:n, :], raw[s][:, n * (j % 2):n * (j % 2) + n, :],
                                         ACT.Copy).then_inc(hi_ready[q], 1)

            def split_on(r, lead=LEAD, next_lead=None):
                split(r, lead, 8)
                split(r + 1, 0, next_lead or lead)

            def pair_hi(t, norm):
                steady(act)
                for c in range(2):
                    ins = nc.scalar.activation(xg_hi[:, bass.ds(t + c, 1), :], x_res[:, bass.ds(t + c, 1), :],
                                               ACT.Copy, scale=gains[:, norm, bass.ds(t + c, 1)])
                ins.then_inc(xg_hi_ready, 1)

            def pair_squares(t, n):
                act.wait_ge(sq_added, n + 1)
                steady(act)
                nc.scalar.activation(pair_tmp[:], x_res[:, bass.ds(t, 2), :], ACT.Square).then_inc(sq_ready, 1)

            def residual_pair(t, norm, n):
                pair_hi(t, norm)
                pair_squares(t, n)

            def rms(name, layer):
                filled(act, name, layer)
                nc.scalar.activation(rstd[:], bank(name, T), ACT.Sqrt, bias=eps,
                                     scale=1.0 / D_MODEL).then_inc(bank_read[BANK_OF[name]], 1)

            def copy_out(dst, name, cols, parts=P, c0=0, done=True):
                ins = nc.scalar.activation(dst, bank(name, cols, parts, c0), ACT.Copy)
                if done:
                    ins.then_inc(bank_read[BANK_OF[name]], 1)
                return ins

            nc.scalar.preload_act_table(ACT.Square)
            load_x(act, 1)
            act.dma_start(cst[:, 0:FIRST_COLS], tables[:, 0:FIRST_COLS]).then_inc(setup_consts, 16)
            load_x(act, 2)
            load_x(act, 3)
            act.dma_start(cst[:, FIRST_COLS:], tables[:, FIRST_COLS:]).then_inc(consts_loaded, 16)
            act.wait_ge(gains_loaded, 16)
            for i in range(4):
                act.wait_ge(x_loaded[i], 16)
                pair_hi(4 * i, 0)
                split(0, i, i + 1)
                pair_hi(4 * i + 2, 0)
            act.wait_ge(setup_consts, 16)
            act.wait_ge(setup_filled, 1)
            nc.scalar.activation(setup_rows[:, 0:XLEN], ps[0:HEADS, 4, 0:XLEN], ACT.Copy).then_inc(bank_read[4], 1)
            nc.scalar.activation(sink_s[:], ps[0:64, 5, 0:DEPTH], ACT.Copy).then_inc(bank_read[5], 1)
            act.drain().then_inc(rows_ready, 1)

            with act.Fori(0, DEPTH) as layer:
                r0 = layer * ROUNDS
                split_on(r0, LEAD + 1, 6)
                rms("rms_mix", layer)
                split(r0 + 1, 6, 8)
                split(r0 + 2, 0, 1)
                act.wait_ge(rp_free, layer * RH + 1)
                filled(act, "k_tok", layer)
                copy_out(kp_tok, "k_tok", PAIR, done=False)
                copy_out(ks_tok, "k_tok", PAIR, NS, PAIR)
                act.drain().then_inc(tok_ready, 1)
                split(r0 + 2, 1, 7)
                filled(act, "v_tok", layer)
                copy_out(v_tok[:], "v_tok", 512)
                split(r0 + 2, 7, 8)
                split(r0 + 3, 0, 1)
                filled(act, "v_tok_s", layer)
                copy_out(v_tok_s[:], "v_tok_s", PAIR, NS)
                act.drain().then_inc(tok_ready, 1)
                split(r0 + 3, 1, 8)
                split(r0 + 4, 0, 8)
                split(r0 + 5, 0, 8)
                split(r0 + 6, 0, GLEAD)

                with act.Fori(0, RH) as g:
                    done = layer * RH + g
                    r = r0 + 6 + g * 4
                    act.wait_ge(qkv_ready, layer * 6 + 6)
                    steady(act)
                    for h in range(2):
                        nc.scalar.activation(q_head[:, h:h + 1, :], qT[:, bass.ds(g + 4 * h, 1), 0:NP], ACT.Copy)
                    for h in range(2):
                        src = qT[:, 4 * h:4 * h + 4, bass.ds(g * 2 * DT + NP, 2 * DT)]
                        ins = nc.scalar.activation(
                            samp_q[:, 32 * h:32 * h + 32].rearrange("p (b h t) -> p b h t", b=2, h=4),
                            src.rearrange("p h (b t) -> p b h t", b=2), ACT.Copy)
                    ins.then_inc(q_staged, 1)
                    split(r, GLEAD, 8)
                    split(r + 1, 0, 1)
                    filled(act, "kcT", layer, g)
                    copy_out(kcT[:], "kcT", 512)

                    def exponentials(h):
                        act.wait_ge(negmax_ready, done * 2 + h + 1)
                        s = stats[:, 12 * h:12 * h + 12]
                        nc.scalar.activation(probs[h][:, 0:P], probs[h][:, 0:P], ACT.Exp, bias=s[:, 2:3],
                                             accum_out=s[:, 4:5])
                        nc.scalar.activation(probs[h][:, P:P + NP], probs[h][:, P:P + NP], ACT.Exp,
                                             bias=s[:, 3:4], accum_out=s[:, 5:6])
                        nc.scalar.activation(s[:, 6:8], s[:, 2:4], ACT.Exp,
                                             bias=s[:, 10:11]).then_inc(exp_ready, 1)

                    def normalise(h):
                        act.wait_ge(sum_inverted, done * 2 + h + 1)
                        s = stats[:, 12 * h:12 * h + 12]
                        nc.scalar.activation(probs[h][:, 0:P], probs[h][:, 0:P], ACT.Copy, scale=s[:, 0:1])
                        nc.scalar.activation(probs[h][:, P:P + NP], probs[h][:, P:P + NP], ACT.Copy,
                                             scale=s[:, 1:2]).then_inc(probs_ready, 1)

                    exponentials(0)
                    split(r + 1, 1, 4)
                    normalise(0)
                    exponentials(1)
                    filled(act, "sampT", layer, g)
                    copy_out(samp_sT[:], "sampT", 64)
                    split(r + 1, 4, 6)
                    normalise(1)
                    filled(act, "pT0", layer, g)
                    copy_out(pT[:], "pT0", NP + P)
                    split(r + 1, 6, 7)
                    act.wait_ge(samp_negmax, done + 1)
                    nc.scalar.activation(samp_p[:], samp_p[:], ACT.Exp, bias=stats[0:64, 21:22],
                                         accum_out=stats[0:64, 22:23])
                    nc.scalar.activation(stats[0:64, 23:24], stats[0:64, 21:22], ACT.Exp,
                                         bias=sink_s[:, bass.ds(layer, 1)]).then_inc(samp_exp, 1)
                    split(r + 1, 7, 8)
                    split(r + 2, 0, 2)

                    def head_hi(h):
                        filled(act, f"pv{h}", layer, g)
                        steady(act)
                        copy_out(cat_hi[:, bass.ds(g + 4 * h, 1), 0:NP], f"pv{h}", NP,
                                 done=False).then_inc(cat_hi_ready, 1)

                    head_hi(0)
                    filled(act, "pT1", layer, g)
                    copy_out(pT[:], "pT1", NP + P)
                    split(r + 2, 2, 5)
                    head_hi(1)
                    split(r + 2, 5, 7)
                    filled(act, "samp_pT", layer, g)
                    copy_out(samp_pT[:], "samp_pT", 64, done=False)
                    copy_out(samp_pnT[:], "samp_pT", 64, NS, 64)
                    split(r + 2, 7, 8)
                    split(r + 3, 0, 1)
                    filled(act, "samp_pv", layer, g)
                    steady(act)
                    for h in range(2):
                        ins = nc.scalar.activation(
                            cat_hi[:, 4 * h:4 * h + 4, bass.ds(g * 2 * DT + NP, 2 * DT)].rearrange(
                                "p h (b t) -> p b h t", b=2),
                            bank("samp_pv", 32, P, 32 * h).rearrange("p (b h t) -> p b h t", b=2, h=4), ACT.Copy)
                    ins.then_inc(cat_hi_ready, 1)
                    split(r + 3, 1, 2)
                    filled(act, "kr_tok", layer, g)
                    steady(act)
                    for b in range(2):
                        ins = nc.scalar.activation(kr_tok[:, b, :], bank("kr_tok", PAIR, P, PAIR * b), ACT.Copy,
                                                   scale=table("kdecay")[:, bass.ds(g * 2 + b, 1)])
                    ins.then_inc(bank_read[BANK_OF["kr_tok"]], 1)
                    split(r + 3, 2, 3)
                    filled(act, "kr_copies", layer, g)
                    steady(act)
                    nc.scalar.activation(k_stack[:], bank("kr_copies", PAIR), ACT.Copy,
                                         scale=table("kdecay_s")[:, bass.ds(g, 1)]).then_inc(k_hi_ready, 1)
                    split(r + 3, 3, 5)
                    filled(act, "vr_tok", layer, g)
                    copy_out(vr_tok[:], "vr_tok", 512)
                    filled(act, "vr_copies", layer, g)
                    nc.scalar.activation(vr_tok_s[:], bank("vr_copies", PAIR, NS), ACT.Copy)
                    nc.scalar.activation(v_stack[:], bank("vr_copies", PAIR), ACT.Copy).then_inc(v_hi_ready, 1)
                    split(r + 3, 5, 7)

                    def own_keys(b0, b1):
                        for b in range(b0, b1):
                            if b >= OWN:
                                filled(act, f"st{b - OWN}", layer, g)
                            nc.scalar.activation(k_own[:, b % OWN, :], k_stack[:].bitcast(F32), ACT.Copy,
                                                 scale=table("own_rows")[:, b:b + 1]).then_inc(own_ready, 1)

                    act.wait_ge(k_stacked, done + 1)
                    own_keys(0, OWN)
                    split(r + 3, 7, 8)
                    for v in range(2):
                        filled(act, f"o{v}", layer, g)
                        ins = nc.scalar.activation(rot_tmp[:, v, :], bank(f"o{v}", T), ACT.Square)
                    ins.then_inc(o_squared, 1)
                    filled(act, "ret_st", layer, g)
                    act.wait_ge(rp_free, done + 1)
                    act.wait_ge(tok_left, layer + 1)
                    copy_out(rp_out[:], "ret_st", 512)
                    act.drain().then_inc(rp_ready, 1)
                    split(r + 4, 0, 1)
                    own_keys(OWN, OWN + 2)
                    split(r + 4, 1, 2)
                    own_keys(OWN + 2, DB)
                    split(r + 4, 2, 4)
                    filled(act, "gnorm", layer, g)
                    nc.scalar.activation(rot_tmp[:, 0, :], bank("gnorm", T), ACT.Sqrt, bias=eps,
                                         scale=1.0 / PAIR).then_inc(bank_read[BANK_OF["gnorm"]], 1)
                    act.wait_ge(gate_raw, done + 1)
                    nc.scalar.activation(gate[:], gate[:], ACT.Silu).then_inc(gate_ready, 1)
                    split(r + 4, 4, GLEAD)
                    act.wait_ge(mixed_ready, done + 1)
                    steady(act)
                    nc.scalar.activation(cat_hi[:, bass.ds(g * 2 + HEADS, 2), :], vr[:],
                                         ACT.Copy).then_inc(cat_hi_ready, 1)

                with act.Fori(0, 4) as i:
                    for c in range(2):
                        split_on(r0 + R_O + i * 2 + c, GLEAD)
                        n = layer * 16 + i * 2 + c
                        act.wait_ge(x_new, n + 1)
                        residual_pair(i * 4 + 2 * c, layer * 2 + 1, n + 8)
                split_on(r0 + R_FFN, GLEAD)
                rms("rms_ffn", layer)
                act.wait_ge(mixer_left, layer + 1)
                steady(act)
                nc.scalar.preload_act_table(ACT.Silu)

                def gate_up(i, t_hi, first=False):
                    r = r0 + R_FFN + i * 2
                    n = layer * (FT // 2) + i
                    if not first:
                        split_on(r)
                        split(r + 1, LEAD, 4)
                    act.wait_ge(ffn_gate, n + 1)
                    nc.scalar.activation(pair_tmp[:], pair_tmp[:], ACT.Silu).then_inc(ffn_silu, 1)
                    split(r + 1, GLEAD if first else 4, 8)
                    split(r + 2, 0, LEAD)
                    act.wait_ge(hid_ready32, n + 1)
                    steady(act)
                    nc.scalar.activation(t_hi, pair_tmp[:], ACT.Copy).then_inc(hid_hi_ready, 1)

                gate_up(0, cat_hi[:, 0:2, :], first=True)
                with act.Fori(1, KT // 2) as i:
                    gate_up(i, cat_hi[:, bass.ds(i * 2, 2), :])
                with act.Fori(0, (FT - KT) // 2) as i:
                    gate_up(i + KT // 2, hid_hi[:, bass.ds(i * 2, 2), :])
                with act.Fori(0, 4) as i:
                    for c in range(2):
                        r = r0 + R_DOWN + i * 6 + 3 * c
                        split(r, LEAD, 8)
                        split(r + 1, 0, 8)
                        split(r + 2, 0, 8, DOWN_ROUNDS[2])
                        split(r + 3, 0, LEAD)
                        n = layer * 16 + 8 + i * 2 + c
                        act.wait_ge(x_new, n + 1)
                        residual_pair(i * 4 + 2 * c, layer * 2 + 2, n + 8)
                split(r0 + ROUNDS, LEAD, LEAD + 1)
            rms("rms_mix", DEPTH)
            for i in range(4):
                act.wait_ge(y_ready, 4 * i + 4)
                act.dma_start(yT.rearrange("(t p) n -> p t n", p=P)[:, 4 * i:4 * i + 4, :],
                              x_res[:, 4 * i:4 * i + 4, :]).then_inc(out_stored, 16)
            act.wait_ge(out_stored, 64)

        @block.vector
        def _(dve):
            def split(r, j0, j1, sizes=FULL):
                for j in range(j0, j1):
                    s, q, n = j // 2, j % 4, sizes[j // 2] // 2
                    dve.wait_ge(hi_ready[q], 2 * r + j // 4 + 1)
                    nc.vector.tensor_tensor(w_lo[q][:, 0:n, :], raw[s][:, n * (j % 2):n * (j % 2) + n, :],
                                            w_hi[q][:, 0:n, :].bitcast(F32),
                                            ALU.subtract).then_inc(split_ready[q], 1)

            def split_on(r, lead=LEAD, next_lead=None):
                split(r, lead, 8)
                split(r + 1, 0, next_lead or lead)

            def lo_of_pair(t, norm, n):
                dve.wait_ge(xg_hi_ready, n + 1)
                for c in range(2):
                    ins = nc.vector.scalar_tensor_tensor(
                        xg_lo[:, bass.ds(t + c, 1), :], x_res[:, bass.ds(t + c, 1), :],
                        gains[:, norm, bass.ds(t + c, 1)],
                        xg_hi[:, bass.ds(t + c, 1), :].bitcast(F32), ALU.mult, ALU.subtract)
                ins.then_inc(xg_ready, 1)

            def reciprocal_std(name, layer):
                copied(dve, name, layer)
                nc.vector.reciprocal(rstd[:], rstd[:])
                dve.drain()

            for q in range(4):
                dve.sem_inc(split_ready[q], CREDIT)
            for a in range(2):
                dve.sem_inc(acc_read[a], 1)
            for b in (6, 7):
                dve.sem_inc(bank_read[b], 1)
            dve.sem_inc(group_used, 1)
            nc.vector.memset(setup_hot[32:33, XLEN:XLEN + HEADS], 1.0).then_inc(setup_done, 1)
            dve.wait_ge(gains_loaded, 16)
            for i in range(4):
                lo_of_pair(4 * i, 0, 2 * i)
                split(0, i, i + 1)
                lo_of_pair(4 * i + 2, 0, 2 * i + 1)
            nc.vector.tensor_tensor(setup_squares[:, 3 * KT // 4:, :], x_res[:, 3 * KT // 4:, :],
                                    x_res[:, 3 * KT // 4:, :], ALU.mult).then_inc(sq_ready, KT // 2)
            dve.wait_ge(consts_loaded, 16)

            with dve.Fori(0, DEPTH) as layer:
                r0 = layer * ROUNDS
                split_on(r0, LEAD + 1, 6)
                reciprocal_std("rms_mix", layer)

                def evacuate(dst, a, r):
                    multiplied(dve, r)
                    return nc.vector.tensor_tensor(dst, acc[a], over_pair(rstd[:]), ALU.mult)

                evacuate(kT[:], 0, r0).then_inc(acc_read[0], 1)
                dve.drain().then_inc(qkv_ready, 1)
                split_on(r0 + 1, 6, LEAD)
                evacuate(vr[:], 1, r0 + 1).then_inc(acc_read[1], 1)
                dve.drain().then_inc(qkv_ready, 1)
                nc.vector.tensor_tensor(cos_std[:], cos, rstd[:], ALU.mult)
                nc.vector.tensor_tensor(sin_std[:], sin, rstd[:], ALU.mult)
                for n in range(4):
                    split_on(r0 + 2 + n)
                    evacuate(qT[:, 2 * n:2 * n + 2, :], n % 2, r0 + 2 + n).then_inc(acc_read[n % 2], 1)
                    dve.drain().then_inc(qkv_ready, 1)
                split(r0 + 6, LEAD, GLEAD)

                with dve.Fori(0, RH) as g:
                    done = layer * RH + g
                    r = r0 + 6 + g * 4

                    def scores(h):
                        filled(dve, f"s{h}", layer, g)
                        if h == 0:
                            dve.wait_ge(group_loaded, done * 48 + 48)
                        s = stats[:, 12 * h:12 * h + 12]
                        nc.vector.tensor_copy(s[:, 10:11], sink_p[:, bass.ds(layer, 1), bass.ds(g + 4 * h, 1)])
                        nc.vector.scalar_tensor_tensor(probs[h][:, 0:P], bank(f"s{h}", P), SCALE,
                                                       biasT[:, h, P:NP], ALU.mult, ALU.add)
                        nc.vector.scalar_tensor_tensor(probs[h][:, P:P + NP], bank(f"s{h}", NP, P, P), SCALE,
                                                       biasT[:, h, :], ALU.mult,
                                                       ALU.add).then_inc(bank_read[BANK_OF[f"s{h}"]], 1)
                        dve.drain()
                        nc.vector.tensor_reduce(s[:, 0:1], probs[h][:, 0:P], AX.X, ALU.max)
                        nc.vector.tensor_reduce(s[:, 1:2], probs[h][:, P:P + NP], AX.X, ALU.max)
                        dve.drain()
                        nc.vector.tensor_scalar(s[:, 2:4], s[:, 0:2], s[:, 10:11], -1.0, ALU.max,
                                                ALU.mult).then_inc(negmax_ready, 1)

                    def invert_sum(h):
                        dve.wait_ge(exp_ready, done * 2 + h + 1)
                        s = stats[:, 12 * h:12 * h + 12]
                        nc.vector.tensor_tensor(s[:, 8:10], s[:, 4:6], s[:, 6:8], ALU.add)
                        dve.drain()
                        nc.vector.reciprocal(s[:, 0:2], s[:, 8:10]).then_inc(sum_inverted, 1)

                    def rotate(x, a, r, scale, r_split):
                        multiplied(dve, r)
                        nc.vector.scalar_tensor_tensor(rot_tmp[:], acc[a], scale, over_pair(cos_std[:]), ALU.mult,
                                                       ALU.mult)
                        nc.vector.scalar_tensor_tensor(pair_tmp[:], acc[a], scale, over_pair(sin_std[:]), ALU.mult,
                                                       ALU.mult).then_inc(acc_read[a], 1)
                        split(r_split, 3, 4)
                        dve.drain()
                        nc.vector.tensor_tensor(x[:, 0, :], rot_tmp[:, 0, :], pair_tmp[:, 1, :], ALU.subtract)
                        nc.vector.tensor_tensor(x[:, 1, :], pair_tmp[:, 0, :], rot_tmp[:, 1, :], ALU.add)

                    def head_lo(h):
                        dve.wait_ge(cat_hi_ready, done * 4 + h + 1)
                        nc.vector.tensor_tensor(cat_lo[:, bass.ds(g + 4 * h, 1), 0:NP], bank(f"pv{h}", NP).unsqueeze(1),
                                                cat_hi[:, bass.ds(g + 4 * h, 1), 0:NP].bitcast(F32),
                                                ALU.subtract).then_inc(bank_read[BANK_OF[f"pv{h}"]], 1)

                    split(r, GLEAD, 7)
                    scores(0)
                    split(r, 7, 8)
                    split(r + 1, 0, 2)
                    scores(1)
                    split(r + 1, 2, 3)
                    invert_sum(0)
                    rotate(q_rot, 0, r, 1.0, r + 1)
                    split(r + 1, 4, 5)
                    dve.drain()
                    nc.vector.tensor_tensor(
                        q_dec[:], q_rot[:, :, NP:T],
                        over_pair(table("qdecay")[:, bass.ds(g * NS, NS)]), ALU.mult).then_inc(qr_ready, 1)
                    invert_sum(1)
                    split(r + 1, 5, 6)
                    filled(dve, "samp_s", layer, g)
                    nc.vector.scalar_tensor_tensor(samp_p[:], bank("samp_s", P + NS, 64), SCALE, bias_s[:],
                                                   ALU.mult, ALU.add).then_inc(bank_read[BANK_OF["samp_s"]], 1)
                    dve.drain()
                    nc.vector.tensor_tensor(samp_p[:, P:P + NS], samp_p[:, P:P + NS],
                                            table("own", 64)[:, bass.ds(g * NS, NS)], ALU.add)
                    dve.drain()
                    nc.vector.tensor_reduce(stats[0:64, 20:21], samp_p[:], AX.X, ALU.max)
                    dve.drain()
                    nc.vector.tensor_scalar(stats[0:64, 21:22], stats[0:64, 20:21],
                                            sink_s[:, bass.ds(layer, 1)], -1.0, ALU.max,
                                            ALU.mult).then_inc(samp_negmax, 1)
                    split(r + 1, 6, 8)
                    dve.wait_ge(samp_exp, done + 1)
                    nc.vector.tensor_tensor(stats[0:64, 20:21], stats[0:64, 22:23], stats[0:64, 23:24], ALU.add)
                    dve.drain()
                    nc.vector.reciprocal(stats[0:64, 22:23], stats[0:64, 20:21])
                    dve.drain()
                    nc.vector.tensor_scalar(samp_p[:], samp_p[:], stats[0:64, 22:23], None,
                                            ALU.mult).then_inc(samp_probs, 1)
                    split(r + 2, 0, 3)
                    rotate(k_rot, 1, r + 1, KSCALE, r + 2)
                    dve.drain()

                    def copies(dst, src):
                        return nc.vector.tensor_copy(
                            dst[:].rearrange("p v (c n) -> p v c n", c=COPIES),
                            src[:, :, NP:T].unsqueeze(2).to_broadcast([P, 2, COPIES, NS]))

                    copies(k_copies, k_rot).then_inc(kr_ready, 1)
                    head_lo(0)
                    split(r + 2, 4, 6)
                    head_lo(1)
                    split(r + 2, 6, 8)
                    dve.wait_ge(cat_hi_ready, done * 4 + 3)
                    for h in range(2):
                        where = [x[:, 4 * h:4 * h + 4, bass.ds(g * 2 * DT + NP, 2 * DT)].rearrange(
                            "p h (b t) -> p b h t", b=2) for x in (cat_lo, cat_hi)]
                        ins = nc.vector.tensor_tensor(
                            where[0], bank("samp_pv", 32, P, 32 * h).rearrange("p (b h t) -> p b h t", b=2, h=4),
                            where[1].bitcast(F32), ALU.subtract)
                    ins.then_inc(bank_read[BANK_OF["samp_pv"]], 1)
                    dve.sem_inc(group_used, 1)
                    split(r + 3, 0, 2)
                    dve.wait_ge(k_hi_ready, done + 1)
                    for p0 in (NS, 3 * NS):
                        ins = nc.vector.scalar_tensor_tensor(
                            k_stack[p0:p0 + NS, :], bank("kr_copies", PAIR, NS, 0, p0),
                            cst[p0:p0 + NS, bass.ds(g + TABLES["kdecay_s"][0], 1)],
                            k_stack[p0:p0 + NS, :].bitcast(F32), ALU.mult, ALU.subtract)
                    ins.then_inc(bank_read[BANK_OF["kr_copies"]], 1)
                    dve.drain().then_inc(k_stacked, 1)
                    split(r + 3, 2, 3)
                    evacuate(vr[:], 0, r + 2).then_inc(acc_read[0], 1)
                    dve.drain()
                    copies(v_copies, vr).then_inc(vr_ready, 1)
                    filled(dve, "ret_s", layer, g)
                    nc.vector.tensor_tensor(ret_sT[:, 0:NP], bank("ret_s", NP),
                                            table("decay")[:, bass.ds(g * NP, NP)], ALU.mult)
                    nc.vector.tensor_tensor(ret_sT[:, NP:NP + P], bank("ret_s", P, P, NP),
                                            table("decay")[:, bass.ds(g * NP, P)], ALU.mult)
                    nc.vector.tensor_tensor(ret_sT[0:NS, NP + P:], bank("ret_s", NS, NS, NP + P),
                                            table("decay_s", NS)[:, bass.ds(g * NS, NS)],
                                            ALU.mult).then_inc(bank_read[BANK_OF["ret_s"]], 1)
                    split(r + 3, 3, 5)
                    dve.wait_ge(v_hi_ready, done + 1)
                    nc.vector.tensor_tensor(v_stack[2 * NS:P, :], bank("vr_copies", PAIR, 2 * NS, 0, 2 * NS),
                                            v_stack[2 * NS:P, :].bitcast(F32),
                                            ALU.subtract).then_inc(bank_read[BANK_OF["vr_copies"]], 1)
                    dve.drain().then_inc(v_stacked, 1)
                    split(r + 3, 5, 7)
                    dve.wait_ge(state_loaded, done * 32 + 32)

                    def update_states(b0, b1):
                        for b in range(b0, b1):
                            filled(dve, f"st{b}", layer, g)
                            s = st[:, 2 * b:2 * b + 2, :]
                            ins = nc.vector.scalar_tensor_tensor(
                                s, s, table("gammaC")[:, bass.ds(g, 1)],
                                bank(f"st{b}", 512).rearrange("p (k n) -> p k n", k=2), ALU.mult,
                                ALU.add)
                            ins.then_inc(bank_read[BANK_OF[f"st{b}"]], 1)

                    update_states(0, 1)
                    split(r + 3, 7, 8)
                    update_states(1, 3)
                    split(r + 4, 0, 1)
                    update_states(3, 5)
                    split(r + 4, 1, 2)
                    update_states(5, 7)
                    split(r + 4, 2, 3)
                    evacuate(gate[:], 1, r + 3).then_inc(acc_read[1], 1)
                    dve.drain().then_inc(gate_raw, 1)
                    split(r + 4, 3, 4)
                    update_states(7, DB)
                    dve.drain().then_inc(st_updated, 1)
                    copied(dve, "gnorm", layer, g)
                    nc.vector.reciprocal(rot_tmp[:, 0, :], rot_tmp[:, 0, :])
                    dve.drain()
                    for v in range(2):
                        nc.vector.tensor_tensor(vr[:, v, :], bank(f"o{v}", T), rot_tmp[:, 0, :],
                                                ALU.mult).then_inc(bank_read[BANK_OF[f"o{v}"]], 1)
                    split(r + 4, 4, 5)
                    dve.drain()
                    dve.wait_ge(gate_ready, done + 1)
                    nc.vector.tensor_tensor(vr[:], vr[:], gate[:], ALU.mult).then_inc(mixed_ready, 1)
                    split(r + 4, 5, GLEAD)
                    dve.wait_ge(cat_hi_ready, done * 4 + 4)
                    nc.vector.tensor_tensor(cat_lo[:, bass.ds(g * 2 + HEADS, 2), :], vr[:],
                                            cat_hi[:, bass.ds(g * 2 + HEADS, 2), :].bitcast(F32),
                                            ALU.subtract).then_inc(cat_ready, 1)

                def add_to_residual(a, r, i, c, n, norm):
                    multiplied(dve, r)
                    xs = x_res[:, bass.ds(i * 4 + 2 * c, 2), :]
                    nc.vector.tensor_tensor(xs, acc[a], xs, ALU.add).then_inc(acc_read[a], 1)
                    dve.drain().then_inc(x_new, 1)
                    lo_of_pair(i * 4 + 2 * c, norm, n)

                with dve.Fori(0, 4) as i:
                    for c in range(2):
                        split_on(r0 + R_O + i * 2 + c, GLEAD)
                        add_to_residual(c, r0 + R_O + i * 2 + c, i, c, layer * 16 + i * 2 + c + 8, layer * 2 + 1)

                split_on(r0 + R_FFN, GLEAD)
                reciprocal_std("rms_ffn", layer)

                def gate_up(i, t_hi, t_lo, first=False):
                    r = r0 + R_FFN + i * 2
                    n = layer * (FT // 2) + i
                    if not first:
                        split_on(r)
                    evacuate(pair_tmp[:], 0, r).then_inc(acc_read[0], 1)
                    dve.drain().then_inc(ffn_gate, 1)
                    split(r + 1, GLEAD if first else 3, 6)
                    dve.wait_ge(ffn_silu, n + 1)
                    nc.vector.tensor_tensor(pair_tmp[:], pair_tmp[:], over_pair(rstd[:]), ALU.mult)
                    split(r + 1, 6, 8)
                    split(r + 2, 0, 3)
                    multiplied(dve, r + 1)
                    nc.vector.tensor_tensor(pair_tmp[:], acc[1], pair_tmp[:], ALU.mult).then_inc(acc_read[1], 1)
                    dve.drain().then_inc(hid_ready32, 1)
                    dve.wait_ge(hid_hi_ready, n + 1)
                    nc.vector.tensor_tensor(t_lo, pair_tmp[:], t_hi.bitcast(F32), ALU.subtract).then_inc(hid_ready, 1)

                gate_up(0, cat_hi[:, 0:2, :], cat_lo[:, 0:2, :], first=True)
                with dve.Fori(1, KT // 2) as i:
                    gate_up(i, cat_hi[:, bass.ds(i * 2, 2), :], cat_lo[:, bass.ds(i * 2, 2), :])
                with dve.Fori(0, (FT - KT) // 2) as i:
                    gate_up(i + KT // 2, hid_hi[:, bass.ds(i * 2, 2), :], hid_lo[:, bass.ds(i * 2, 2), :])

                with dve.Fori(0, 4) as i:
                    for c in range(2):
                        r = r0 + R_DOWN + i * 6 + 3 * c
                        split(r, LEAD, 8)
                        split(r + 1, 0, 8)
                        split(r + 2, 0, 8, DOWN_ROUNDS[2])
                        split(r + 3, 0, LEAD)
                        add_to_residual(c, r + 2, i, c, layer * 16 + 8 + i * 2 + c + 8, layer * 2 + 2)
                split(r0 + ROUNDS, LEAD, LEAD + 1)

            reciprocal_std("rms_mix", DEPTH)
            for t in range(KT):
                nc.vector.scalar_tensor_tensor(x_res[:, t, :], x_res[:, t, :], gains[:, 2 * DEPTH, t:t + 1],
                                               rstd[:], ALU.mult, ALU.mult).then_inc(y_ready, 1)

        @block.tensor
        def _(pe):
            def products(r, a, x_hi, x_lo, kt0=0, kt_x=0, j0=0, j1=8, sizes=FULL, kts=KT, ready=None,
                         beside=None):
                for j in range(j0, j1):
                    s, q, n = j // 2, j % 4, sizes[j // 2] // 2
                    k0 = kt0 + sum(sizes[0:s]) + n * (j % 2)
                    if ready is not None:
                        ready(k0, n)
                    pe.wait_ge(split_ready[q], 2 * r + j // 4 + 1 + CREDIT)
                    for t in range(n):
                        k = k0 + t
                        x = k - kt0 + kt_x
                        for c in range(2):
                            cols = slice(P * c, P * c + P)
                            out = acc[a][:, c, :]
                            nc.tensor.matmul(out, w_hi[q][:, t, cols], x_hi[:, x, :], start=(k == 0),
                                             stop=False, skip_group_check=True)
                            nc.tensor.matmul(out, w_hi[q][:, t, cols], x_lo[:, x, :], start=False,
                                             stop=False, skip_group_check=True)
                            ins = nc.tensor.matmul(out, w_lo[q][:, t, cols], x_hi[:, x, :], start=False,
                                                   stop=(k == kts - 1), skip_group_check=True)
                            if t == n - 1 and c == 1:
                                ins.then_inc(ring_used[q], 1)
                            if beside is not None:
                                beside(4 * (j - j0) + 2 * t + c)

            def acc_free(a, layer, pair):
                pe.wait_ge(acc_read[a], layer * PAIRS_PER_ACC + pair + 1)

            def sum_partitions(name, layer, parts, group=0):
                free(pe, name, layer, group)
                for n, x in enumerate(parts):
                    ins = nc.tensor.matmul(bank(name, T), ones, x, start=(n == 0), stop=(n == len(parts) - 1))
                ins.then_inc(bank_filled[BANK_OF[name]], 1)

            for q in range(4):
                pe.sem_inc(ring_used[q], 1)
            pe.sem_inc(down_done, 1)
            pe.wait_ge(setup_done, 1)
            pe.wait_ge(setup_loaded, 48)
            pe.wait_ge(setup_consts, 16)
            nc.tensor.matmul(ps[0:HEADS, 4, 0:XLEN], setup_hot[:, XLEN:XLEN + HEADS], setup_hot[:, 0:XLEN],
                             start=True, stop=True)
            nc.tensor.matmul(ps[0:64, 5, 0:DEPTH], table("head_rows", HEADS), setup_rows[:, XLEN:XLEN + DEPTH],
                             start=True, stop=True).then_inc(setup_filled, 1)

            with pe.Fori(0, DEPTH) as layer:
                r0 = layer * ROUNDS

                def in_pair(r, a, n, j0=0, j1=8, first=False, beside=None):
                    def ready(k0, size):
                        pe.wait_ge(xg_ready, layer * 16 + (k0 + size) // 2)
                    if j0 == 0:
                        acc_free(a, layer, n)
                    products(r, a, xg_hi, xg_lo, j0=j0, j1=j1, ready=ready if first else None,
                             beside=beside)

                in_pair(r0, 0, 0, first=True)
                in_pair(r0 + 1, 1, 0, 0, 2)
                pe.wait_ge(sq_added, layer * 16 + 8 + 1)
                sum_partitions("rms_mix", layer, [sq_acc[:]])
                in_pair(r0 + 1, 1, 0, 2, 6)
                pe.wait_ge(qkv_ready, layer * 6 + 1)
                free(pe, "k_tok", layer)
                for kv in range(KV):
                    nc.tensor.transpose(bank("k_tok", P, P, P * kv), kT[:, kv, P:NP], ident)
                    ins = nc.tensor.transpose(bank("k_tok", P, NS, PAIR + P * kv), kT[:, kv, NP:T], ident)
                ins.then_inc(bank_filled[BANK_OF["k_tok"]], 1)
                in_pair(r0 + 1, 1, 0, 6, 8)
                in_pair(r0 + 2, 0, 1, 0, 4)
                pe.wait_ge(qkv_ready, layer * 6 + 2)
                free(pe, "v_tok", layer)
                for b in range(2):
                    for kv in range(KV):
                        ins = nc.tensor.transpose(bank("v_tok", P, P, PAIR * b + P * kv), vr[:, kv, P * b:P * b + P],
                                                  ident)
                ins.then_inc(bank_filled[BANK_OF["v_tok"]], 1)
                in_pair(r0 + 2, 0, 1, 4, 6)
                free(pe, "v_tok_s", layer)
                for kv in range(KV):
                    ins = nc.tensor.transpose(bank("v_tok_s", P, NS, P * kv), vr[:, kv, NP:T], ident)
                ins.then_inc(bank_filled[BANK_OF["v_tok_s"]], 1)
                in_pair(r0 + 2, 0, 1, 6, 8)
                for n in range(1, 4):
                    in_pair(r0 + 2 + n, n % 2, 1 + n // 2)

                with pe.Fori(0, RH) as g:
                    done = layer * RH + g
                    r = r0 + 6 + g * 4
                    pair = g * 2 + 3

                    def fill(name):
                        free(pe, name, layer, g)

                    def is_filled(ins, name):
                        ins.then_inc(bank_filled[BANK_OF[name]], 1)

                    def scores(h):
                        fill(f"s{h}")
                        nc.tensor.matmul(bank(f"s{h}", P), q_head[:, h, 0:P], kT[:, h, 0:P], start=True, stop=True)
                        is_filled(nc.tensor.matmul(bank(f"s{h}", NP, P, P), q_head[:, h, P:NP], kT[:, h, 0:NP],
                                                   start=True, stop=True), f"s{h}")

                    def transpose_probs(h):
                        pe.wait_ge(probs_ready, done * 2 + h + 1)
                        fill(f"pT{h}")
                        for b in range(3):
                            ins = nc.tensor.transpose(bank(f"pT{h}", P, P, P * b), probs[h][:, P * b:P * b + P], ident)
                        is_filled(ins, f"pT{h}")

                    def values(h):
                        copied(pe, f"pT{h}", layer, g)
                        fill(f"pv{h}")
                        v = [v_tok[:, b, P * h:P * h + P] for b in range(2)]
                        nc.tensor.matmul(bank(f"pv{h}", P), v[0], pT[:, 0:P], start=True, stop=True)
                        nc.tensor.matmul(bank(f"pv{h}", P, P, P), v[0], pT[:, P:NP], start=True, stop=False)
                        is_filled(nc.tensor.matmul(bank(f"pv{h}", P, P, P), v[1], pT[:, NP:NP + P], start=False,
                                                   stop=True), f"pv{h}")

                    in_pair(r, 0, pair, 0, 6)
                    pe.wait_ge(q_staged, done + 1)
                    scores(0)
                    pe.wait_ge(group_loaded, done * 48 + 48)
                    fill("kcT")
                    for b in range(2):
                        for kv in range(KV):
                            ins = nc.tensor.transpose(bank("kcT", P, P, PAIR * b + P * kv),
                                                      kc[:, b, P * kv:P * kv + P], ident)
                    is_filled(ins, "kcT")
                    in_pair(r, 0, pair, 6, 7)
                    scores(1)
                    in_pair(r, 0, pair, 7, 8)
                    in_pair(r + 1, 1, pair, 0, 1)
                    copied(pe, "kcT", layer, g)
                    fill("sampT")
                    for kv in range(KV):
                        for b in range(2):
                            c0 = 32 * kv + 16 * b
                            ins = nc.tensor.matmul(bank("sampT", 16, P, c0), kcT[:, 2 * b + kv, :],
                                                   samp_q[:, c0:c0 + 16], start=True, stop=True)
                    is_filled(ins, "sampT")
                    in_pair(r + 1, 1, pair, 1, 4)
                    transpose_probs(0)
                    copied(pe, "sampT", layer, g)
                    fill("samp_s")
                    steady(pe)
                    nc.tensor.transpose(bank("samp_s", P, 64), samp_sT[:], ident)
                    for kv in range(KV):
                        ins = nc.tensor.matmul(bank("samp_s", NS, 32, P, 32 * kv), samp_q[:, 32 * kv:32 * kv + 32],
                                               kT[:, kv, NP:T], start=True, stop=True)
                    is_filled(ins, "samp_s")
                    in_pair(r + 1, 1, pair, 4, 7)
                    values(0)
                    transpose_probs(1)
                    in_pair(r + 1, 1, pair, 7, 8)
                    in_pair(r + 2, 0, pair + 1, 0, 2)
                    values(1)
                    in_pair(r + 2, 0, pair + 1, 2, 3)
                    pe.wait_ge(samp_probs, done + 1)
                    fill("samp_pT")
                    steady(pe)
                    nc.tensor.transpose(bank("samp_pT", 64), samp_p[:, 0:P], ident[0:64, 0:64])
                    is_filled(nc.tensor.transpose(bank("samp_pT", 64, NS, 64), samp_p[:, P:P + NS],
                                                  ident[0:64, 0:64]), "samp_pT")

                    def state_times_q(v, n):
                        b, d = n // 2, n % 2
                        nc.tensor.matmul(bank(f"o{v}", DT, P, NP + DT * b), st[:, 2 * b + d, P * v:P * v + P],
                                         q_dec[:, d, DT * b:DT * b + DT], start=(n == 0), stop=False,
                                         skip_group_check=True)

                    pe.wait_ge(qr_ready, done + 1)
                    pe.wait_ge(state_loaded, done * 32 + 32)
                    fill("o0")
                    in_pair(r + 2, 0, pair + 1, 3, 5, beside=lambda n: state_times_q(0, n))
                    copied(pe, "samp_pT", layer, g)
                    fill("samp_pv")
                    for kv in range(KV):
                        nc.tensor.matmul(bank("samp_pv", 32, P, 32 * kv), v_tok_s[:, P * kv:P * kv + P],
                                         samp_pnT[:, 32 * kv:32 * kv + 32], start=(kv == 0), stop=False,
                                         skip_group_check=True)
                        for b in range(2):
                            c0 = 32 * kv + 16 * b
                            ins = nc.tensor.matmul(bank("samp_pv", 16, P, c0), vc[:, b, P * kv:P * kv + P],
                                                   samp_pT[:, c0:c0 + 16], start=False, stop=True,
                                                   skip_group_check=True)
                    is_filled(ins, "samp_pv")
                    in_pair(r + 2, 0, pair + 1, 5, 6, beside=lambda n: state_times_q(0, n + 8))
                    pe.wait_ge(kr_ready, done + 1)
                    fill("kr_tok")
                    for b in range(2):
                        for d in range(2):
                            ins = nc.tensor.transpose(bank("kr_tok", P, P, PAIR * b + P * d),
                                                      k_rot[:, d, P * b:P * b + P], ident)
                    is_filled(ins, "kr_tok")
                    in_pair(r + 2, 0, pair + 1, 6, 7, beside=lambda n: state_times_q(0, n + 12))
                    fill("kr_copies")
                    for d in range(2):
                        ins = nc.tensor.transpose(bank("kr_copies", P, P, P * d), k_copies[:, d, :], ident)
                    is_filled(ins, "kr_copies")
                    fill("o1")
                    in_pair(r + 2, 0, pair + 1, 7, 8, beside=lambda n: state_times_q(1, n))
                    fill("ret_s")
                    for c0, n, m0, n0 in ((0, NP, 0, 0), (NP, P, P, P)):
                        for d in range(2):
                            nc.tensor.matmul(bank("ret_s", n, P, c0), k_rot[:, d, m0:m0 + P],
                                             q_rot[:, d, n0:n0 + n], start=(d == 0), stop=(d == 1))
                    for d in range(2):
                        ins = nc.tensor.matmul(bank("ret_s", NS, NS, NP + P), k_rot[:, d, NP:T], q_rot[:, d, NP:T],
                                               start=(d == 0), stop=(d == 1))
                    is_filled(ins, "ret_s")
                    in_pair(r + 3, 1, pair + 1, 0, 2, beside=lambda n: state_times_q(1, n + 4))
                    pe.wait_ge(vr_ready, done + 1)
                    fill("vr_tok")
                    for b in range(2):
                        for d in range(2):
                            ins = nc.tensor.transpose(bank("vr_tok", P, P, PAIR * b + P * d),
                                                      vr[:, d, P * b:P * b + P], ident)
                    is_filled(ins, "vr_tok")
                    fill("vr_copies")
                    for d in range(2):
                        ins = nc.tensor.transpose(bank("vr_copies", P, P, P * d), v_copies[:, d, :], ident)
                    is_filled(ins, "vr_copies")
                    in_pair(r + 3, 1, pair + 1, 2, 3, beside=lambda n: state_times_q(1, n + 12))
                    in_pair(r + 3, 1, pair + 1, 3, 4)

                    copied(pe, "ret_s", layer, g)
                    copied(pe, "vr_tok", layer, g)
                    pe.wait_ge(v_hi_ready, done + 1)
                    for v in range(2):
                        dims = slice(P * v, P * v + P)
                        name = f"o{v}"
                        nc.tensor.matmul(bank(name, NP), vr_tok[:, 0, dims], ret_sT[:, 0:NP], start=False,
                                         stop=False, skip_group_check=True)
                        nc.tensor.matmul(bank(name, P, P, P), vr_tok[:, 1, dims], ret_sT[:, NP:NP + P],
                                         start=False, stop=False, skip_group_check=True)
                        is_filled(nc.tensor.matmul(bank(name, NS, P, NP), vr_tok_s[:, dims],
                                                   ret_sT[0:NS, NP + P:], start=False, stop=True,
                                                   skip_group_check=True), name)
                    fill("ret_st")
                    for d in range(2):
                        for b in range(2):
                            ins = nc.tensor.matmul(bank("ret_st", PAIR, P, PAIR * d), kr_tok[:, b, P * d:P * d + P],
                                                   vr_tok[:, b, :], start=(b == 0), stop=(b == 1))
                    is_filled(ins, "ret_st")

                    def keys_times_values(b0, b1):
                        for b in range(b0, b1):
                            pe.wait_ge(own_ready, done * DB + b + 1)
                            fill(f"st{b}")
                            for d in range(2):
                                ins = nc.tensor.matmul(bank(f"st{b}", PAIR, P, PAIR * d),
                                                       k_own[:, b % OWN, P * d:P * d + P], v_stack[:], start=True,
                                                       stop=True)
                            is_filled(ins, f"st{b}")

                    pe.wait_ge(v_stacked, done + 1)
                    keys_times_values(0, 1)
                    in_pair(r + 3, 1, pair + 1, 4, 5)
                    keys_times_values(1, 3)
                    in_pair(r + 3, 1, pair + 1, 5, 6)
                    keys_times_values(3, 5)
                    in_pair(r + 3, 1, pair + 1, 6, 7)
                    keys_times_values(5, 7)
                    in_pair(r + 3, 1, pair + 1, 7, 8)
                    keys_times_values(7, DB)
                    pe.wait_ge(o_squared, done + 1)
                    sum_partitions("gnorm", layer, [rot_tmp[:, v, :] for v in range(2)], g)

                copied(pe, "samp_pv", layer, RH - 1)
                pe.wait_ge(cat_ready, layer * RH + RH - 1)

                def cat_wait(k0, size):
                    if k0 + size == KT:
                        pe.wait_ge(cat_ready, layer * RH + RH)

                acc_free(0, layer, P_O // 2)
                products(r0 + R_O, 0, cat_hi, cat_lo, ready=cat_wait)
                acc_free(1, layer, P_O // 2)
                products(r0 + R_O + 1, 1, cat_hi, cat_lo)
                with pe.Fori(1, 4) as i:
                    for c in range(2):
                        acc_free(c, layer, i + P_O // 2)
                        products(r0 + R_O + i * 2 + c, c, cat_hi, cat_lo)

                def ffn_ready(k0, size):
                    pe.wait_ge(xg_ready, layer * 16 + 8 + (k0 + size) // 2)

                acc_free(0, layer, P_FFN // 2)
                products(r0 + R_FFN, 0, xg_hi, xg_lo, ready=ffn_ready)
                acc_free(1, layer, P_FFN // 2)
                products(r0 + R_FFN + 1, 1, xg_hi, xg_lo, j1=2)
                pe.wait_ge(sq_added, layer * 16 + 16 + 1)
                sum_partitions("rms_ffn", layer, [sq_acc[:]])
                products(r0 + R_FFN + 1, 1, xg_hi, xg_lo, j0=2)
                with pe.Fori(1, FT // 2) as i:
                    for c in range(2):
                        acc_free(c, layer, i + P_FFN // 2)
                        products(r0 + R_FFN + i * 2 + c, c, xg_hi, xg_lo)

                def hid_wait(k0, size):
                    pe.wait_ge(hid_ready, layer * (FT // 2) + (k0 + size + 1) // 2)

                with pe.Fori(0, 4) as i:
                    for c in range(2):
                        acc_free(c, layer, i + P_DOWN // 2)
                        r = r0 + R_DOWN + i * 6 + 3 * c
                        products(r, c, cat_hi, cat_lo, kts=FT, ready=hid_wait)
                        products(r + 1, c, hid_hi, hid_lo, 16, 0, kts=FT, ready=hid_wait)
                        products(r + 2, c, hid_hi, hid_lo, 32, 16, sizes=DOWN_ROUNDS[2], kts=FT, ready=hid_wait)
                pe.sem_inc(down_done, 1)
            pe.wait_ge(sq_added, DEPTH * 16 + 8 + 1)
            sum_partitions("rms_mix", DEPTH, [sq_acc[:]])

        @block.gpsimd
        def _(pool):
            st_tiles = st[:].rearrange("p (b k) v -> p b k v", b=DB)

            def add_squares(n):
                pool.wait_ge(sq_ready, n + 1)
                nc.gpsimd.tensor_tensor(sq_acc[:], sq_acc[:], pair_tmp[:, 0, :], ALU.add)
                pool.drain()
                nc.gpsimd.tensor_tensor(sq_acc[:], sq_acc[:], pair_tmp[:, 1, :], ALU.add)
                pool.drain().then_inc(sq_added, 1)

            pool.dma_start(setup_hot[:, 0:XLEN], onehot).then_inc(setup_loaded, 16)
            pool.dma_start(setup_hot[0:32, XLEN:XLEN + HEADS], rel_bias).then_inc(setup_loaded, 16)
            with nc.allow_non_contiguous_dma(reason="16 sinks"):
                pool.dma_start(setup_rows[:, XLEN:XLEN + DEPTH], sinksT).then_inc(setup_loaded, 16)
            pool.dma_start(sink_p[:], sinks.rearrange("(o l) h -> o l h", o=1).to_broadcast([P, DEPTH, HEADS])
                           ).then_inc(bias_s_loaded, 16)
            pool.sem_inc(sq_added, 1)
            pool.sem_inc(rp_free, 1)
            first = setup_squares[:, 0:4, :]
            for i in range(4):
                part = slice(4 * i, 4 * i + 4)
                if i < 3:
                    pool.wait_ge(x_loaded[i], 16)
                    nc.gpsimd.tensor_tensor(setup_squares[:, part, :], x_res[:, part, :], x_res[:, part, :], ALU.mult)
                else:
                    pool.wait_ge(sq_ready, KT // 2)
                pool.drain()
                if i > 0:
                    nc.gpsimd.tensor_tensor(first, first, setup_squares[:, part, :], ALU.add)
                    pool.drain()
            nc.gpsimd.tensor_tensor(first[:, 0:2, :], first[:, 0:2, :], first[:, 2:4, :], ALU.add)
            pool.drain()
            nc.gpsimd.tensor_tensor(sq_acc[:], first[:, 0, :], first[:, 1, :], ALU.add)
            pool.drain().then_inc(sq_added, KT // 2)
            pool.wait_ge(rows_ready, 1)
            pool.dma_start(bass.AP(bias_rows, 0, [[P * XLEN, HEADS], [XLEN, P], [1, XLEN]]),
                           setup_rows[:, 0:XLEN].unsqueeze(1).to_broadcast([HEADS, P, XLEN])
                           ).then_inc(rows_stored, 16)
            pool.wait_ge(rows_stored, 16)

            def shifted(head, col, dims):
                return bass.AP(bias_rows, head * (P * XLEN) + (P - 1 + col), dims)

            for b in range(2):
                for h in range(HEADS):
                    row = (h // 4) * 32 + b * 16 + (h % 4) * DT
                    pool.dma_start(bias_s[row:row + DT, 0:P],
                                   shifted(h, 0, [[XLEN - 1, DT], [1, P]])).then_inc(bias_s_loaded, 16)
                    pool.dma_start(bias_s[row:row + DT, P:P + NS].rearrange("p (b t) -> p b t", b=DB),
                                   shifted(h, P, [[XLEN - 1, DT], [0, DB], [1, DT]])).then_inc(bias_s_loaded, 16)
            pool.wait_ge(bias_s_loaded, 16 + 2 * 2 * HEADS * 16)
            for w_new, w_old in ((new_ks, cache_k), (new_vs, cache_v)):
                pool.dma_start(w_new[:, :, 0:WIN - DT].rearrange("l b w k d -> (l b) (w k d)"),
                               w_old[:, :, DT:WIN].rearrange("l b w k d -> (l b) (w k d)")).then_inc(state_stored, 16)

            with pool.Fori(0, DEPTH) as layer:
                pool.wait_ge(down_done, layer + 1)
                pool.wait_ge(tok_ready, layer * 2 + 1)
                steady(pool)
                rows = new_ks[bass.ds(layer, 1)].rearrange("l b w k d -> (l b) w (k d)")
                vrows = new_vs[bass.ds(layer, 1)].rearrange("l b w k d -> (l b) w (k d)")
                pool.dma_start(new_kp[bass.ds(layer, 1)].rearrange("l o w k d -> (l o w) (k d)"),
                               kp_tok).then_inc(tok_stored, 16)
                for b in range(DB):
                    pool.dma_start(rows[b, WIN - DT:WIN, :], ks_tok[DT * b:DT * b + DT, :]).then_inc(tok_stored, 16)
                pool.wait_ge(tok_ready, layer * 2 + 2)
                steady(pool)
                pool.dma_start(new_vp[bass.ds(layer, 1)].rearrange("l o w k d -> (l o w) (k d)"),
                               v_tok[:, 1, :]).then_inc(tok_stored, 16)
                for b in range(DB):
                    pool.dma_start(vrows[b, WIN - DT:WIN, :], v_tok_s[DT * b:DT * b + DT, :]).then_inc(tok_stored, 16)

                pool.wait_ge(tok_stored, layer * 32 * (1 + DB) + 32 * (1 + DB))
                pool.sem_inc(tok_left, 1)

                def load_group(g):
                    pool.wait_ge(group_used, layer * RH + g + 1)
                    steady(pool)
                    pool.dma_start(biasT[:], shifted(g, 0, [[XLEN - 1, P], [4 * P * XLEN, 2], [1, NP]])
                                   ).then_inc(group_loaded, 16)
                    for dst, src in ((kc, cache_k), (vc, cache_v)):
                        pool.dma_start(dst[:], src[bass.ds(layer, 1), bass.ds(g * 2, 2)].rearrange(
                            "l b w k d -> w (l b) (k d)")).then_inc(group_loaded, 16)

                def move_states(g, last=False):
                    done = layer * RH + g

                    def head_rows(states, k):
                        return states[bass.ds(layer, 1), :, bass.ds(g, 1), P * k:P * k + P, :].rearrange(
                            "l b r p v -> p (l b r) v")

                    pool.wait_ge(state_stored, done * 32 + 32)
                    steady(pool)
                    for k in range(2):
                        pool.dma_start(st_tiles[:, :, k, :], head_rows(state, k)).then_inc(state_loaded, 16)
                    if not last:
                        load_group(g + 1)
                    pool.wait_ge(rp_ready, done + 1)
                    steady(pool)
                    pool.dma_start(new_rp[bass.ds(layer, 1), :, bass.ds(g, 1)].rearrange(
                        "l o r (k p) v -> p (l o r k) v", p=P), rp_out[:]).then_inc(rp_stored, 16)
                    pool.wait_ge(rp_stored, done * 16 + 16)
                    pool.sem_inc(rp_free, 1)
                    pool.wait_ge(st_updated, done + 1)
                    steady(pool)
                    for k in range(2):
                        pool.dma_start(head_rows(new_rs, k), st_tiles[:, :, k, :]).then_inc(state_stored, 16)

                load_group(0)
                with pool.Fori(0, RH - 1) as g:
                    move_states(g)
                move_states(RH - 1, last=True)

                pool.wait_ge(state_stored, layer * RH * 32 + RH * 32 + 32)
                pool.sem_inc(mixer_left, 1)
                for part in range(2):
                    if part == 0:
                        copied(pool, "rms_mix", layer)
                    else:
                        copied(pool, "rms_ffn", layer)
                    steady(pool)
                    nc.gpsimd.memset(sq_acc[:], 0.0)
                    pool.drain()
                    with pool.Fori(0, KT // 2) as i:
                        add_squares(layer * 16 + 8 * part + 8 + i)


def shape_tables():
    import numpy as np

    f = np.float32
    cst = np.zeros((P, TABLE_COLS), f)

    def put(name, value, parts=P):
        a, b = TABLES[name]
        cst[0:parts, a:b] = np.asarray(value, np.float64).reshape(-1, b - a) if np.ndim(value) else value

    put("ident", np.eye(P))
    put("ones", 1.0)
    put("eps", EPS)
    gamma = 1.0 - 2.0 ** (-5.0 - np.arange(RH))
    put("gammaC", gamma ** DT)
    tok = np.arange(P)
    put("kdecay", np.stack([gamma[h] ** (NP - 1.0 - (tok + P * b)) for h in range(RH) for b in range(2)], 1))
    inv = f(1.0) / (f(10000.0) ** np.linspace(0.0, 1.0, P, dtype=f)).astype(f)
    pos = np.concatenate([np.arange(NP), np.tile(2048 + np.arange(DT), DB)]).astype(f)
    angle = (pos[None, :] * inv[:, None]).astype(f).astype(np.float64)
    put("cos", np.cos(angle))
    put("sin", np.sin(angle))
    n = np.arange(NP)[None, :] - tok[:, None]
    put("decay", np.concatenate([np.where(n >= 0, gamma[h] ** np.maximum(n, 0), 0.0) for h in range(RH)], 1))
    row = np.arange(NS)
    put("qdecay", np.concatenate([gamma[h] ** (row % DT + 1.0) for h in range(RH)]))
    n = row[None, :] - row[:, None]
    same = row[None, :] // DT == row[:, None] // DT
    put("decay_s", np.concatenate([np.where(same & (n >= 0), gamma[h] ** np.maximum(n, 0), 0.0)
                                   for h in range(RH)], 1), NS)
    tiled = np.arange(P) % NS
    put("kdecay_s", np.stack([gamma[h] ** (DT - 1.0 - tiled % DT) for h in range(RH)], 1))
    put("own_rows", tiled[:, None] // DT == np.arange(DB)[None, :])
    batch = (np.arange(64) // 16) % 2
    put("own", np.concatenate([np.where(row[None, :] // DT == 2 * g + batch[:, None], 0.0, -1e30)
                               for g in range(4)], 1), 64)
    rows_head = (np.arange(64) // 32) * 4 + (np.arange(64) % 16) // DT
    put("head_rows", np.arange(HEADS)[:, None] == rows_head[None, :], HEADS)

    delta = NP - 1 - np.arange(XLEN)
    d = np.maximum(delta, 1).astype(f)
    large = 16 + (np.log(d / f(16)).astype(f) / f(np.log(8.0)) * f(16)).astype(np.int32)
    bucket = np.where(delta < 16, np.maximum(delta, 0), np.minimum(large, 31))
    valid = (delta >= 0) & (delta < WIN)
    hot = np.zeros((33, XLEN), f)
    hot[bucket[valid], np.nonzero(valid)[0]] = 1.0
    hot[32, ~valid] = -1e30
    return cst, hot


def kernel(x_prompt, x_sample, cache_k_win, cache_v_win, state_ret, rel_bias, w_in, sinks, w_o, norm_mix,
           norm_ffn, w_gate_up, w_down, norm_final):
    import numpy as np
    import concourse.bacc as bacc
    from concourse.bass_utils import run_bass_kernel_spmd

    cst, hot = shape_tables()
    x = np.concatenate([np.asarray(x_prompt).reshape(NP, D_MODEL), np.asarray(x_sample).reshape(NS, D_MODEL)])
    gains = np.stack([g for l in range(DEPTH) for g in (np.asarray(norm_mix)[l], np.asarray(norm_ffn)[l])]
                     + [np.asarray(norm_final)])
    ins = {
        "xT": x.T, "cache_k": cache_k_win, "cache_v": cache_v_win, "state": state_ret, "rel_bias": rel_bias,
        "w_in": w_in, "sinks": sinks, "sinksT": np.asarray(sinks).T, "w_o": w_o,
        "gainsT": gains.reshape(2 * DEPTH + 1, KT, P).transpose(2, 0, 1), "w_gate_up": w_gate_up,
        "w_down": w_down, "tables": cst, "onehot": hot,
    }
    ins = {k: np.ascontiguousarray(v) for k, v in ins.items()}
    outs = {
        "yT": (D_MODEL, T), "new_kp": (DEPTH, 1, WIN, KV, P), "new_vp": (DEPTH, 1, WIN, KV, P),
        "new_rp": (DEPTH, 1, RH, PAIR, PAIR), "new_ks": (DEPTH, DB, WIN, KV, P), "new_vs": (DEPTH, DB, WIN, KV, P),
        "new_rs": (DEPTH, DB, RH, PAIR, PAIR),
    }
    nc = bacc.Bacc("TRN2", target_bir_lowering=False, num_devices=1)
    aps = [nc.dram_tensor(k, v.shape, mybir.dt.from_np(v.dtype), kind="ExternalInput").ap() for k, v in ins.items()]
    aps += [nc.dram_tensor(k, shape, F32, kind="ExternalOutput").ap() for k, shape in outs.items()]
    hybrid_trunk(nc, *aps)
    r = run_bass_kernel_spmd(nc, [ins], core_ids=[0]).results[0]
    y = np.ascontiguousarray(r["yT"].T)
    return (y[0:NP].reshape(1, NP, D_MODEL), y[NP:T].reshape(DB, DT, D_MODEL), r["new_kp"], r["new_vp"],
            r["new_rp"], r["new_ks"], r["new_vs"], r["new_rs"])
```
